# Optimizing a Trainium2 kernel written in Bass

```python
import jax, jax.numpy as jnp
from jax import lax
import numpy as np

D_MODEL = 1024
BATCH = 1
SEQ = 256
DEPTH = 2
DEC_BATCH = 8
DEC_SEQ = 4
PAST_LEN = 2048
PAGE_SIZE = 128

GLA_HEADS = 4
GLA_DK = D_MODEL // 2
GLA_DV = D_MODEL
GLA_HDK = GLA_DK // GLA_HEADS
GLA_HDV = GLA_DV // GLA_HEADS
GLA_GATE_RANK = 16
GLA_TAU = 16.0
GLA_CHUNK = 64
GLA_SPLITS = [GLA_DK, 2 * GLA_DK, 2 * GLA_DK + GLA_DV, 2 * GLA_DK + 2 * GLA_DV]
GLA_IN = 2 * GLA_DK + 2 * GLA_DV + GLA_GATE_RANK
D_RNN = 1280
RG_BLOCKS = 8
RG_BLOCK = D_RNN // RG_BLOCKS
CONV_W = 4
RG_C = 8.0
PEER_HEADS = 8
PEER_NKEYS = 128
PEER_N = PEER_NKEYS * PEER_NKEYS
PEER_DQ = 256
PEER_DHALF = PEER_DQ // 2
PEER_TOPK = 16
PEER_TOKEN_BLOCK = 256
EPS = 1e-6
N_GLA = (DEPTH + 1) // 2
N_RG = DEPTH // 2

kernel_name = 'hybrid_gla_rglru_peer_step'

def rms_norm(x, gain):
    xf = x.astype(jnp.float32)
    y = xf * lax.rsqrt(jnp.mean(xf * xf, axis=-1, keepdims=True) + EPS)
    return (y * gain.astype(jnp.float32)).astype(x.dtype)

def gla_mixer(h, s0, w_in, w_gate2, b_gate, onorm_g, w_out):
    B, L, _ = h.shape
    f32 = jnp.float32
    q, k, v, g, lr = jnp.split(h @ w_in, GLA_SPLITS, axis=-1)
    log_a = jax.nn.log_sigmoid((lr @ w_gate2 + b_gate).astype(f32)) / GLA_TAU

    def heads(t, d):
        return t.astype(f32).reshape(B, L, GLA_HEADS, d).transpose(0, 2, 1, 3)

    q = heads(q, GLA_HDK) * (GLA_HDK ** -0.5)
    k = heads(k, GLA_HDK)
    v = heads(v, GLA_HDV)
    log_a = heads(log_a, GLA_HDK)
    C = min(GLA_CHUNK, L)
    n = -(-L // C)
    pad = n * C - L

    def to_chunks(t):
        t = jnp.pad(t, ((0, 0), (0, 0), (0, pad), (0, 0)))
        return t.reshape(B, GLA_HEADS, n, C, t.shape[-1]).transpose(2, 0, 1, 3, 4)

    causal = jnp.tril(jnp.ones((C, C), dtype=bool))

    def chunk_step(S, blk):
        qi, ki, vi, ai = blk
        b = jnp.cumsum(ai, axis=2)
        qd = qi * jnp.exp(b)
        kd = ki * jnp.exp(-b)
        scores = jnp.where(causal, jnp.einsum('bhtd,bhsd->bhts', qd, kd), 0.0)
        o = jnp.einsum('bhts,bhsv->bhtv', scores, vi) + jnp.einsum('bhtd,bhdv->bhtv', qd, S)
        b_end = b[:, :, -1, :]
        k_end = ki * jnp.exp(b_end[:, :, None, :] - b)
        S = S * jnp.exp(b_end)[..., None] + jnp.einsum('bhsd,bhsv->bhdv', k_end, vi)
        return S, o

    S, o = lax.scan(chunk_step, s0.astype(f32), (to_chunks(q), to_chunks(k), to_chunks(v), to_chunks(log_a)))
    o = o.transpose(1, 2, 0, 3, 4).reshape(B, GLA_HEADS, n * C, GLA_HDV)[:, :, :L]
    o = rms_norm(o, onorm_g)
    o = o.transpose(0, 2, 1, 3).reshape(B, L, GLA_DV) * jax.nn.silu(g.astype(f32))
    return o.astype(h.dtype) @ w_out, S.astype(s0.dtype)

def rglru_mixer(h, start, h0, conv0, w_in, conv_w, conv_b, w_a, b_a, w_x, b_x, lam, w_out):
    B, L, _ = h.shape
    f32 = jnp.float32
    y_br, x_br = jnp.split(h @ w_in, [D_RNN], axis=-1)
    xc = jnp.concatenate([conv0.astype(x_br.dtype), x_br], axis=1)
    xconv = conv_b + sum(xc[:, j:j + L] * conv_w[j] for j in range(CONV_W))
    new_conv = xc[:, L:]
    xf = xconv.astype(f32)
    xb = xf.reshape(B, L, RG_BLOCKS, RG_BLOCK)
    gate_r = jax.nn.sigmoid(jnp.einsum('blni,nio->blno', xb, w_a.astype(f32)).reshape(B, L, D_RNN) + b_a)
    gate_i = jax.nn.sigmoid(jnp.einsum('blni,nio->blno', xb, w_x.astype(f32)).reshape(B, L, D_RNN) + b_x)
    log_a = -RG_C * gate_r * jax.nn.softplus(-lam.astype(f32))
    reset = ((start + jnp.arange(L)) == 0)[None, :, None]
    a = jnp.where(reset, 0.0, jnp.exp(log_a))
    mult = jnp.where(reset, 1.0, jnp.sqrt(-jnp.expm1(2.0 * log_a)))
    bx = mult * gate_i * xf

    def combine(left, right):
        return (left[0] * right[0], right[0] * left[1] + right[1])

    a_cum, b_cum = lax.associative_scan(combine, (a, bx), axis=1)
    hs = a_cum * h0.astype(f32)[:, None, :] + b_cum
    out = (hs * jax.nn.gelu(y_br.astype(f32))).astype(h.dtype) @ w_out
    return out, hs[:, -1].astype(h0.dtype), new_conv.astype(conv0.dtype)

def peer_mixer(h, w_q, sub_keys, u_tab, v_tab):
    B, L, D = h.shape
    T = B * L
    nb = -(-T // PEER_TOKEN_BLOCK)
    xt = jnp.pad(h.reshape(T, D), ((0, nb * PEER_TOKEN_BLOCK - T), (0, 0))).reshape(nb, PEER_TOKEN_BLOCK, D)
    f32 = jnp.float32

    def block(xb):
        tb = xb.shape[0]
        q = (xb @ w_q).astype(f32).reshape(tb, PEER_HEADS, 2, PEER_DHALF)
        s = jnp.einsum('thpd,hpnd->thpn', q, sub_keys.astype(f32))
        s_top, i_top = lax.top_k(s, PEER_TOPK)
        cand = (s_top[:, :, 0, :, None] + s_top[:, :, 1, None, :]).reshape(tb, PEER_HEADS, PEER_TOPK * PEER_TOPK)
        cidx = (i_top[:, :, 0, :, None] * PEER_NKEYS + i_top[:, :, 1, None, :]).reshape(tb, PEER_HEADS, PEER_TOPK * PEER_TOPK)
        best, pos = lax.top_k(cand, PEER_TOPK)
        idx = jnp.take_along_axis(cidx, pos, axis=-1)
        g = jax.nn.softmax(best, axis=-1)
        act = jax.nn.gelu(jnp.einsum('thkd,td->thk', u_tab[idx], xb).astype(f32))
        wgt = (g * act).astype(xb.dtype)
        return jnp.einsum('thk,thkd->td', wgt, v_tab[idx])

    out = lax.map(block, xt).reshape(nb * PEER_TOKEN_BLOCK, D)[:T]
    return out.reshape(B, L, D)

def trunk(x, c, start, gla_s0, rg_h0, rg_conv0, p):
    B = x.shape[0]
    gla_new, rg_h_new, rg_conv_new = [], [], []
    cond = jax.nn.silu(c)
    for i in range(DEPTH):
        mod = (cond @ p['ada_w'][i] + p['ada_b'][i]).astype(x.dtype).reshape(B, 6, D_MODEL)
        sh1, sc1, g1, sh2, sc2, g2 = [mod[:, j, None, :] for j in range(6)]
        hm = rms_norm(x, p['norm_mix_g'][i]) * (1 + sc1) + sh1
        j = i // 2
        if i % 2 == 0:
            mixed, s_new = gla_mixer(hm, gla_s0[j], p['gla_w_in'][j], p['gla_w_gate2'][j], p['gla_b_gate'][j],
                                     p['gla_onorm_g'][j], p['gla_w_out'][j])
            gla_new.append(s_new)
        else:
            mixed, h_new, conv_new = rglru_mixer(hm, start, rg_h0[j], rg_conv0[j], p['rg_w_in'][j], p['rg_conv_w'][j],
                                                 p['rg_conv_b'][j], p['rg_w_a'][j], p['rg_b_a'][j], p['rg_w_x'][j],
                                                 p['rg_b_x'][j], p['rg_lambda'][j], p['rg_w_out'][j])
            rg_h_new.append(h_new)
            rg_conv_new.append(conv_new)
        x = x + g1 * mixed
        hm = rms_norm(x, p['norm_ffn_g'][i]) * (1 + sc2) + sh2
        x = x + g2 * peer_mixer(hm, p['peer_w_q'][i], p['peer_sub_keys'][i], p['peer_u'][i], p['peer_v'][i])
    y = rms_norm(x, p['final_norm_g'])
    return y, jnp.stack(gla_new), jnp.stack(rg_h_new), jnp.stack(rg_conv_new)

def setup_inputs(seed: int = 0) -> dict:
    key = jax.random.key(seed)
    ks = iter(jax.random.split(key, 40))
    f32 = jnp.float32

    def nrm(shape, scale):
        return jax.random.normal(next(ks), shape, f32) * scale

    def gain(shape):
        return 1.0 + nrm(shape, 0.01)

    lam_u = jax.random.uniform(next(ks), (N_RG, D_RNN), f32, 0.9, 0.999)
    lam_p = lam_u ** (1.0 / RG_C)
    rg_lambda = jnp.log(lam_p) - jnp.log1p(-lam_p)
    return {
        'x_prompt': nrm((BATCH, SEQ, D_MODEL), 1.0),
        'x_sample': nrm((DEC_BATCH, DEC_SEQ, D_MODEL), 1.0),
        'c_prompt': nrm((BATCH, D_MODEL), 1.0),
        'c_sample': nrm((DEC_BATCH, D_MODEL), 1.0),
        'state_gla': nrm((N_GLA, DEC_BATCH, GLA_HEADS, GLA_HDK, GLA_HDV), 1.0),
        'state_rglru_h': nrm((N_RG, DEC_BATCH, D_RNN), 0.5),
        'state_rglru_conv': nrm((N_RG, DEC_BATCH, CONV_W - 1, D_RNN), 1.0),
        'ada_w': nrm((DEPTH, D_MODEL, 6 * D_MODEL), 0.5 * D_MODEL ** -0.5),
        'ada_b': nrm((DEPTH, 6 * D_MODEL), 0.01),
        'norm_mix_g': gain((DEPTH, D_MODEL)),
        'norm_ffn_g': gain((DEPTH, D_MODEL)),
        'gla_w_in': nrm((N_GLA, D_MODEL, GLA_IN), D_MODEL ** -0.5),
        'gla_w_gate2': nrm((N_GLA, GLA_GATE_RANK, GLA_DK), GLA_GATE_RANK ** -0.5),
        'gla_b_gate': nrm((N_GLA, GLA_DK), 0.01),
        'gla_onorm_g': gain((N_GLA, GLA_HDV)),
        'gla_w_out': nrm((N_GLA, GLA_DV, D_MODEL), GLA_DV ** -0.5),
        'rg_w_in': nrm((N_RG, D_MODEL, 2 * D_RNN), D_MODEL ** -0.5),
        'rg_conv_w': nrm((N_RG, CONV_W, D_RNN), CONV_W ** -0.5),
        'rg_conv_b': nrm((N_RG, D_RNN), 0.01),
        'rg_w_a': nrm((N_RG, RG_BLOCKS, RG_BLOCK, RG_BLOCK), RG_BLOCK ** -0.5),
        'rg_b_a': nrm((N_RG, D_RNN), 0.01),
        'rg_w_x': nrm((N_RG, RG_BLOCKS, RG_BLOCK, RG_BLOCK), RG_BLOCK ** -0.5),
        'rg_b_x': nrm((N_RG, D_RNN), 0.01),
        'rg_lambda': rg_lambda,
        'rg_w_out': nrm((N_RG, D_RNN, D_MODEL), D_RNN ** -0.5),
        'peer_w_q': nrm((DEPTH, D_MODEL, PEER_HEADS * PEER_DQ), D_MODEL ** -0.5),
        'peer_sub_keys': nrm((DEPTH, PEER_HEADS, 2, PEER_NKEYS, PEER_DHALF), PEER_DHALF ** -0.5),
        'peer_u': nrm((DEPTH, PEER_N, D_MODEL), D_MODEL ** -0.5),
        'peer_v': nrm((DEPTH, PEER_N, D_MODEL), 0.5),
        'final_norm_g': gain((D_MODEL,)),
    }

def reference(x_prompt, x_sample, c_prompt, c_sample, state_gla, state_rglru_h, state_rglru_conv,
              ada_w, ada_b, norm_mix_g, norm_ffn_g, gla_w_in, gla_w_gate2, gla_b_gate, gla_onorm_g, gla_w_out,
              rg_w_in, rg_conv_w, rg_conv_b, rg_w_a, rg_b_a, rg_w_x, rg_b_x, rg_lambda, rg_w_out,
              peer_w_q, peer_sub_keys, peer_u, peer_v, final_norm_g):
    p = dict(ada_w=ada_w, ada_b=ada_b, norm_mix_g=norm_mix_g, norm_ffn_g=norm_ffn_g,
             gla_w_in=gla_w_in, gla_w_gate2=gla_w_gate2, gla_b_gate=gla_b_gate, gla_onorm_g=gla_onorm_g,
             gla_w_out=gla_w_out, rg_w_in=rg_w_in, rg_conv_w=rg_conv_w, rg_conv_b=rg_conv_b, rg_w_a=rg_w_a,
             rg_b_a=rg_b_a, rg_w_x=rg_w_x, rg_b_x=rg_b_x, rg_lambda=rg_lambda, rg_w_out=rg_w_out,
             peer_w_q=peer_w_q, peer_sub_keys=peer_sub_keys, peer_u=peer_u, peer_v=peer_v,
             final_norm_g=final_norm_g)
    dt = x_prompt.dtype
    gla0 = jnp.zeros((N_GLA, BATCH, GLA_HEADS, GLA_HDK, GLA_HDV), state_gla.dtype)
    h0 = jnp.zeros((N_RG, BATCH, D_RNN), state_rglru_h.dtype)
    conv0 = jnp.zeros((N_RG, BATCH, CONV_W - 1, D_RNN), state_rglru_conv.dtype)
    y_prompt, gla_p, h_p, conv_p = trunk(x_prompt, c_prompt.astype(dt), 0, gla0, h0, conv0, p)
    y_sample, gla_s, h_s, conv_s = trunk(x_sample, c_sample.astype(x_sample.dtype), PAST_LEN,
                                         state_gla, state_rglru_h, state_rglru_conv, p)
    return (y_prompt, y_sample, gla_p, gla_s, h_p, h_s, conv_p, conv_s)


_drawn_inputs = setup_inputs


def setup_inputs(seed=0):
    import zlib

    import numpy as np

    out = dict(_drawn_inputs(seed))
    spreads = {}
    factors = {'norm_mix_g': 4.28,
     'norm_ffn_g': 36.24,
     'gla_b_gate': 8.0,
     'gla_onorm_g': 33.163,
     'rg_b_a': 42.868,
     'rg_b_x': 31.961,
     'final_norm_g': 32.801,
     'rg_conv_b': 4.758}
    for name, (base, spread) in spreads.items():
        noise = np.random.default_rng([zlib.crc32(name.encode()), seed]).standard_normal(out[name].shape)
        drawn = base * np.exp(spread * noise) if base else spread * noise
        out[name] = __import__('jax').numpy.asarray(drawn.astype(out[name].dtype))
    for name, factor in factors.items():
        out[name] = (out[name] * factor).astype(out[name].dtype)
    return out
```

```python
from contextlib import ExitStack

import concourse.bass as bass
from concourse import mybir

F32 = mybir.dt.float32
F32R = mybir.dt.float32r
U32 = mybir.dt.uint32
ALU = mybir.AluOpType
ACT = mybir.ActivationFunctionType
AX_X = mybir.AxisListType.X

P = 128
D = 1024
KD = D // P
SEQ = 256
NB, NT = 8, 4
T = SEQ + NB * NT
NSEQ = 1 + NB
EPS = 1e-6
HEADS, HDV = 4, 256
CH = 64
NCH = SEQ // CH
TAU = 16.0
RANK = 16
DR = 1280
RT = DR // P
PH, TOPK, NKEY = 8, 16, 128
SLOTS = PH * TOPK
GRP = 8
NGRP = NKEY // GRP
HALF = NKEY // 2
LOWEST = -3.0e38
RING = 4

PAR_COLS = {}
_at = 0
for _name, _n in (("ada_b", 96), ("mix_g", 16), ("ffn_g", 16), ("final_g", 8), ("b_gate", 4), ("onorm_g", 2),
                  ("lam", RT), ("b_a", RT), ("b_x", RT), ("conv_w", 4 * RT), ("conv_b", RT)):
    PAR_COLS[_name] = (_at, _at + _n)
    _at += _n
PAR_N = _at
CON_COLS = {}
_at = 0
for _name, _n in (("ident", 128), ("iota", 128), ("keep", T), ("causal", CH), ("sample_causal", 32), ("seq_mask", NB)):
    CON_COLS[_name] = (_at, _at + _n)
    _at += _n
CON_N = _at

GATE_PAIRS = [[(0, 0), (1, 0), (0, 1), (1, 1), (2, 1), (1, 2), (2, 2), (3, 2)],
              [(2, 3), (3, 3), (4, 3), (3, 4), (4, 4)]]

SEGMENTS = [("ada0", 48, "raw"), ("gla_in", 24, "split"), ("gla_out", 8, "split"), ("wq0", 16, "split"),
            ("ada1", 48, "raw"), ("uv0", 256, "split"), ("rg_in", 20, "split"), ("gates", 8, "raw"),
            ("rg_out", 8, "split"), ("wq1", 16, "split"), ("uv1", 256, "split")]
STREAM, SPLIT, BANKED = {}, {}, {}
_n = _m = _u = 0
for _name, _c, _kind in SEGMENTS:
    STREAM[_name], SPLIT[_name], BANKED[_name] = _n, _m, _u
    _n += _c
    _m += _c if _kind == "split" else 0
    _u += {"uv0": 128, "uv1": 128, "gates": 2 * RT}.get(_name, _c)


def build_step(nc, xt, ct, par, con, ada, gla_in, w_lr, w_gate2, gla_out, wq, keys, u_tab, v_tab, rg_in, gates,
               rg_out, rg_tail, gla_state, h_state, conv_state,
               y_out, gla_p_out, gla_s_out, h_out, conv_p_out, conv_s_out):
    with ExitStack() as ctx:
        def sb(name, shape, dt=F32):
            return ctx.enter_context(nc.sbuf_tensor(name, shape, dt))

        def sem(name):
            return ctx.enter_context(nc.semaphore(name))

        x = sb("x", [P, KD, T])
        hid = sb("hid", [P, KD, T])
        hid_hi = sb("hid_hi", [P, KD, T], F32R)
        hid_lo = sb("hid_lo", [P, KD, T], F32R)
        raw = sb("raw", [P, RING, D])
        w_hi = sb("w_hi", [P, 2, D], F32R)
        w_lo = sb("w_lo", [P, 2, D], F32R)
        wgt_hi = sb("wgt_hi", [P, 2, GRP, T], F32R)
        wgt_lo = sb("wgt_lo", [P, 2, GRP, T], F32R)
        wgt = sb("wgt", [P, T])
        gel = sb("gel", [P, 2, T])
        mod = sb("mod", [P, 2, 6, KD, NSEQ])
        parm = sb("parm", [P, PAR_N])
        const = sb("const", [P, CON_N])
        cond = sb("cond", [P, KD, NSEQ])
        coef = sb("coef", [P, KD, NSEQ])
        ones = sb("ones", [P, P])
        mean = sb("mean", [P, T])
        root = sb("root", [P, T])
        newt = sb("newt", [P, T])
        arena = sb("arena", [P, 21504])

        def area(at, *dims, dt=F32, parts=P):
            n = 1
            for d in dims:
                n *= d
            v = arena[0:parts, at:at + n]
            if dt != F32:
                v = v.bitcast(dt)
            if len(dims) == 2:
                return v.rearrange("p (a b) -> p a b", a=dims[0])
            if len(dims) == 3:
                return v.rearrange("p (a b c) -> p a b c", a=dims[0], b=dims[1])
            return v

        proj = area(0, 24, T)
        q, k = proj[:, 0:4, :], proj[:, 4:8, :]
        vt, gt = proj[:, 8:16, :], proj[:, 16:24, :]
        ot = vt
        mix_g = area(0, KD, T)
        decay = area(6912, HEADS, T)
        e_pos = area(8064, HEADS, T)
        e_neg = area(9216, HEADS, T)
        k_end = area(10368, HEADS, T)
        lr_t = area(10368, T, parts=RANK)
        lr_w = area(18432, KD, RANK)
        gate2 = area(18432 + KD * RANK, 4 * P, parts=RANK)
        v_tok = area(11520, 5, D)
        ke_tok = area(16640, 5, 512)
        sc = area(19200, NCH * HEADS, CH, parts=CH)
        sc_s = area(20224, HEADS, 32, parts=32)
        s_pr = area(20352, HEADS, HDV)
        ke_m = area(6912, 2, 512, parts=32)
        s_in = area(9216, 2, D)
        rms_h = area(0, HEADS, T)
        rms_t = area(1152, HEADS, T)
        yb = area(0, RT, T)
        xb = area(2880, RT, T)
        xc = area(5760, RT, T)
        g_r = area(8640, RT, T)
        g_i = area(11520, RT, T)
        av = area(14400, RT, T)
        mult = xb
        xs = area(17280, RT, NB, 7)
        h0 = area(17840, RT, NB)
        conv0 = area(17920, RT, NB, 3)
        tail = area(18160, 2, D)
        sp = area(20208, 8, RT)
        tmp_s = area(20320, RT, NB, NT)
        hl_out = area(20640, RT, NSEQ)
        cs_out = area(20736, RT, NB, 3)
        cp_out = area(20976, RT, 3)
        mix_r = area(8640, KD, T)
        qp = area(0, 16, T)
        key = area(4608, 16, NKEY)
        scor = area(6656, 3, 16, NKEY)
        cand = area(12800, PH, 256)
        onek = area(14848, SLOTS, TOPK)
        val = area(16896, 16, TOPK)
        idx = area(17152, 16, TOPK, dt=U32)
        idx_f = area(17408, 16, TOPK)
        best = area(17664, PH, TOPK)
        pos = area(17792, PH, TOPK, dt=U32)
        pa_f = area(17920, SLOTS)
        pb_f = area(18048, SLOTS)
        pa = area(18176, SLOTS, dt=U32)
        pb = area(18304, SLOTS, dt=U32)
        g_mat = area(0, HALF, T)
        sel = area(18432, 3, T)
        oh_b = area(19296, 2, 4, NKEY)
        oh_a = area(20320, 2, 4, HALF)
        slot = area(20832, 3, SLOTS)
        ssum = area(21216, 2, PH)

        def pcol(name, a=0, b=None):
            lo, hi = PAR_COLS[name]
            return parm[:, lo + a:hi if b is None else lo + b]

        def ccol(name, parts=P):
            lo, hi = CON_COLS[name]
            return const[0:parts, lo:hi]

        ident, iota = ccol("ident"), ccol("iota")

        pu = ctx.enter_context(nc.psum_tensor("pu", [P, 4, 512], F32))
        pm = ctx.enter_context(nc.psum_tensor("pm", [P, 4, 512], F32))
        pv, pg = pm[:, 0:2, :], pm[:, 2:4, :]

        raw_full = [sem(f"raw_full{s}") for s in range(RING)]
        hi_done = sem("hi_done")
        lo_done = sem("lo_done")
        split_used = sem("split_used")
        raw_used = sem("raw_used")
        gate_used = sem("gate_used")
        pu_evac = sem("pu_evac")
        pv_evac = sem("pv_evac")
        vec = sem("vec")
        act_own = sem("act_own")
        (consts_in, ones_set, cond_ready, side_in, sq_ready, sum_ready, mean_ready, root_ready, hid_ready, hh_ready,
         hl_ready) = [sem(n) for n in (
            "consts_in", "ones_set", "cond_ready", "side_in", "sq_ready", "sum_ready", "mean_ready", "root_ready",
            "hid_ready", "hh_ready", "hl_ready")]
        (lr_ready, lrt_ready, z_ready, absz_ready, minz_ready, log_ready, cum_ready, exps_ready, dend_ready,
         edend_ready, ke_ready, qk_ready, tr_ready, tr_evac, sc_ready, sc_masked, o_ready, o_evac, ds_ready, s_new,
         kem_ready, st_used, stn_ready, osq_ready, osum_ready, omean_ready, oroot_ready, silu_ready,
         og_ready, gla_p_done) = [sem(n) for n in (
            "lr_ready", "lrt_ready", "z_ready", "absz_ready", "minz_ready", "log_ready", "cum_ready", "exps_ready",
            "dend_ready", "edend_ready", "ke_ready", "qk_ready", "tr_ready", "tr_evac", "sc_ready", "sc_masked",
            "o_ready", "o_evac", "ds_ready", "s_new", "kem_ready", "st_used", "stn_ready", "osq_ready",
            "osum_ready", "omean_ready", "oroot_ready", "silu_ready", "og_ready", "gla_p_done")]
        st_in = [sem(f"st_in{s}") for s in range(2)]
        st_out = [sem(f"st_out{s}") for s in range(2)]
        (rg_side, conv_ready, tanh_ready, sqrt_ready, sp_ready, gelu_y, lame_ready, hs_ready, hg_ready) = [
            sem(n) for n in ("rg_side", "conv_ready", "tanh_ready", "sqrt_ready", "sp_ready", "gelu_y",
                             "lame_ready", "hs_ready", "hg_ready")]
        (key_in, s_ready, s_evac, shift_ready, exp_ready, slot_ready, slot_t, sel_ready, oh_ready, oh_used, g_evac,
         gel_used, wh_ready, w_ready, out_ready, outs_done) = [sem(n) for n in (
            "key_in", "s_ready", "s_evac", "shift_ready", "exp_ready", "slot_ready", "slot_t", "sel_ready",
            "oh_ready", "oh_used", "g_evac", "gel_used", "wh_ready", "w_ready", "out_ready", "outs_done")]
        MOVING = {"gla_in": 1, "gla_out": 2, "wq0": 3, "uv0": 3, "rg_in": 4, "rg_out": 5, "wq1": 6, "uv1": 6}

        srcs = {"ada0": ada[0], "ada1": ada[1], "gla_in": gla_in, "gla_out": gla_out, "wq0": wq[0], "wq1": wq[1],
                "rg_in": rg_in, "gates": gates, "rg_out": rg_out}
        counts = {name: c for name, c, _ in SEGMENTS}
        kinds = {name: kind for name, _, kind in SEGMENTS}
        order = [name for name, _, _ in SEGMENTS]
        GATE_OUTS = [3, 5]

        def freed(eng, name, c):
            if name == "gates":
                eng.wait_ge(gate_used, 5 * (c // 2) + GATE_OUTS[c % 2])
            elif kinds[name] == "split":
                eng.wait_ge(lo_done, SPLIT[name] + c + 1)
            else:
                eng.wait_ge(raw_used, (0 if name == "ada0" else counts["ada0"]) + c + 1)

        block = ctx.enter_context(nc.Block())

        @block.sync
        def _(sp_):
            for n, name in enumerate(order):
                total = counts[name]
                for s in range(RING):
                    if n:
                        freed(sp_, order[n - 1], counts[order[n - 1]] - RING + s)
                    src = u_tab[int(name[2]), s] if name[:2] == "uv" else srcs[name][s]
                    sp_.dma_start(raw[:, s, :], src).then_inc(raw_full[s], 16)
                if name == "gates":
                    for c in range(RING, total):
                        freed(sp_, name, c - RING)
                        sp_.dma_start(raw[:, c % RING, :], srcs[name][c]).then_inc(raw_full[c % RING], 16)
                elif name[:2] == "uv":
                    lay = int(name[2])
                    for c in range(RING, GRP):
                        freed(sp_, name, c - RING)
                        sp_.dma_start(raw[:, c % RING, :], u_tab[lay, c]).then_inc(raw_full[c % RING], 16)
                    with sp_.Fori(0, (total - 2 * GRP) // RING) as i:
                        for s in range(RING):
                            freed(sp_, name, i * RING + GRP - RING + s)
                            src = u_tab[lay, i * 2 + GRP + s // 2] if s % 2 == 0 else v_tab[lay, i * 2 + s // 2]
                            sp_.dma_start(raw[:, s, :], src).then_inc(raw_full[s], 16)
                    for c in range(GRP):
                        freed(sp_, name, total - GRP - RING + c)
                        sp_.dma_start(raw[:, c % RING, :], v_tab[lay, NKEY - GRP + c]).then_inc(raw_full[c % RING], 16)
                elif total > RING:
                    with sp_.Fori(1, total // RING) as i:
                        for s in range(RING):
                            freed(sp_, name, (i - 1) * RING + s)
                            sp_.dma_start(raw[:, s, :], srcs[name][i * RING + s]).then_inc(raw_full[s], 16)

        @block.gpsimd
        def _(pool):
            pool.memset(ones[:], 1.0).then_inc(ones_set, 1)
            pool.wait_ge(edend_ready, 1)
            pool.wait_ge(qk_ready, 1)
            pool.wait_ge(tr_evac, 15)
            for b in range(2):
                pool.dma_start(s_in[:, b, :], gla_state[b]).then_inc(st_in[b], 16)
            for b in range(NB):
                pool.wait_ge(stn_ready, HEADS * (b + 1))
                pool.dma_start(gla_s_out[b], s_in[:, b % 2, :]).then_inc(st_out[b % 2], 16)
                if b + 2 < NB:
                    pool.wait_ge(st_out[b % 2], 16 * (b // 2 + 1))
                    pool.dma_start(s_in[:, b % 2, :], gla_state[b + 2]).then_inc(st_in[b % 2], 16)
            pool.wait_ge(s_new, HEADS * NCH)
            pool.dma_start(gla_p_out, s_pr).then_inc(gla_p_done, 16)
            pool.wait_ge(og_ready, 1)
            pool.dma_start(key, keys[0]).then_inc(key_in, 16)
            pool.wait_ge(w_ready, NKEY)
            pool.dma_start(h0, h_state).then_inc(rg_side, 16)
            pool.dma_start(conv0, conv_state).then_inc(rg_side, 16)
            pool.dma_start(tail, rg_tail).then_inc(rg_side, 16)
            pool.wait_ge(hs_ready, 1)
            pool.dma_start(h_out, hl_out).then_inc(outs_done, 16)
            pool.dma_start(conv_s_out, cs_out).then_inc(outs_done, 16)
            pool.dma_start(conv_p_out, cp_out).then_inc(outs_done, 16)
            pool.dma_start(key, keys[1]).then_inc(key_in, 16)
            pool.wait_ge(out_ready, 1)
            pool.dma_start(y_out, hid[:]).then_inc(outs_done, 16)
            pool.wait_ge(outs_done, 16 * 4)
            pool.wait_ge(gla_p_done, 16)
            pool.wait_ge(st_out[0], 16 * NB // 2)
            pool.wait_ge(st_out[1], 16 * NB // 2)

        @block.scalar
        def _(act):
            own = [0]

            def link(ins):
                own[0] += 1
                ins.then_inc(act_own, 1)
                act.wait_ge(act_own, own[0])

            act.dma_start(cond[:], ct).then_inc(consts_in, 16)
            act.dma_start(parm[:], par).then_inc(consts_in, 16)
            act.dma_start(x[:], xt).then_inc(consts_in, 16)
            act.dma_start(const[:], con).then_inc(consts_in, 16)
            act.dma_start(lr_w, w_lr).then_inc(side_in, 16)
            act.dma_start(gate2, w_gate2).then_inc(side_in, 16)
            act.wait_ge(consts_in, 64)
            act.activation(cond[:], cond[:], ACT.Silu).then_inc(cond_ready, 1)

            def ada_out(lay, first, last):
                before = lay * counts["ada0"]
                flat = mod[:, lay].rearrange("p j k s -> p (j k) s")
                with act.Fori(first // 4, last // 4) as i:
                    for s in range(4):
                        act.wait_ge(raw_used, i * 4 + before + s + 1)
                        act.activation(flat[:, i * 4 + s, :], pu[:, s, 0:NSEQ], ACT.Identity,
                                       bias=pcol("ada_b")[:, bass.ds(i * 4 + lay * 48 + s, 1)]).then_inc(pu_evac, 1)

            def high(s4, s2, full):
                act.wait_ge(raw_full[s4], full)
                act.activation(w_hi[:, s2, :], raw[:, s4, :], ACT.Copy).then_inc(hi_done, 1)

            def project(name, dest):
                total, m0, n0 = counts[name], SPLIT[name], STREAM[name]

                def group(i, first):
                    for s in range(4):
                        if not first or m0 + s >= 2:
                            act.wait_ge(split_used, i * 4 + (m0 + s - 1))
                        if not (first and s < 2):
                            act.activation(dest[:, i * 4 + (s - 2), :], pu[:, (s - 2) % 4, 0:T], ACT.Copy).then_inc(pu_evac, 1)
                        high(s, s % 2, i * 16 + (n0 // RING + 1) * 16)

                group(0, True)
                if total > 4:
                    with act.Fori(1, total // 4) as i:
                        group(i, False)
                for s in range(2):
                    act.wait_ge(split_used, m0 + total - 1 + s)
                    act.activation(dest[:, total - 2 + s, :], pu[:, 2 + s, 0:T], ACT.Copy).then_inc(pu_evac, 1)

            def norm_root(n):
                act.wait_ge(mean_ready, n + 1)
                act.activation(root[:], mean[:], ACT.Sqrt).then_inc(root_ready, 1)
                if n < 4:
                    act.wait_ge(hid_ready, n + 1)
                    act.activation(hid_hi[:], hid[:], ACT.Copy).then_inc(hh_ready, 1)

            def peer(lay):
                project(f"wq{lay}", qp)
                for tt in range(3):
                    rows = P if tt < 2 else 32
                    for b in range(4):
                        act.wait_ge(s_ready, lay * 12 + tt * 4 + b + 1)
                        act.activation(scor[0:rows, tt, 4 * b:4 * b + 4, :],
                                       pm[0:rows, b, :].rearrange("p (a n) -> p a n", a=4), ACT.Copy).then_inc(s_evac, 1)
                for tt in range(3):
                    rows = P if tt < 2 else 32
                    if lay == 0:
                        ada_out(1, tt * 16, tt * 16 + 16)
                    act.wait_ge(shift_ready, lay * 3 + tt + 1)
                    act.activation(slot[0:rows, 2, :], slot[0:rows, 2, :], ACT.Exp).then_inc(exp_ready, 1)

                name = f"uv{lay}"
                m0, n0, full0 = SPLIT[name], lay * NKEY, (STREAM[name] // RING + 1) * 16

                def g_out(hf):
                    view = g_mat.rearrange("p i t -> p t i")
                    with act.Fori(0, T // 16) as i:
                        for b in range(2):
                            act.wait_ge(oh_used, i * 4 + ((lay * 2 + hf) * (T // 4) + b * 2 + 2))
                            act.activation(view[:, bass.ds(i * 16 + b * 8, 8), :],
                                           pg[:, b, :].rearrange("p (t i) -> p t i", t=8), ACT.Copy).then_inc(g_evac, 1)

                def gelu(n, bank):
                    if not isinstance(n, int) or n >= 2:
                        act.wait_ge(gel_used, n - 1)
                    act.activation(gel[:, bank % 2, :], pu[:, bank, 0:T], ACT.Gelu_apprx_tanh).then_inc(pu_evac, 1)

                def pair_group(g):
                    for j in range(GRP):
                        m = g * 16 + (m0 + GRP - 16 + 2 * j)
                        full = g * 64 + (full0 + 32 - 64 + 16 * (j // 2))
                        act.wait_ge(split_used, m - 1)
                        if j:
                            gelu(g * 8 + (n0 + j - 1), (j - 1) % 4)
                        high((2 * j) % 4, 0, full)
                        act.wait_ge(split_used, m)
                        high((2 * j + 1) % 4, 1, full)
                    act.wait_ge(split_used, m + 1)
                    gelu(g * 8 + (n0 + GRP - 1), 3)

                g_out(0)
                for j in range(GRP):
                    act.wait_ge(split_used, m0 + j - 1)
                    if j:
                        act.wait_ge(split_used, m0 + j)
                        gelu(n0 + j - 1, (j - 1) % 4)
                    high(j % 4, j % 2, full0 + 16 * (j // 4))
                act.wait_ge(split_used, m0 + GRP)
                gelu(n0 + GRP - 1, 3)
                pair_group(1)
                with act.Fori(1, 4) as i:
                    pair_group(i * 2)
                    pair_group(i * 2 + 1)
                act.wait_ge(gel_used, n0 + HALF)
                g_out(1)
                with act.Fori(4, 8) as i:
                    pair_group(i * 2)
                    pair_group(i * 2 + 1)
                for j in range(GRP):
                    act.wait_ge(split_used, m0 + 248 + j - 1)
                    high(j % 4, j % 2, full0 + 16 * (62 + j // 4))

            ada_out(0, 0, 48)
            norm_root(0)
            project("gla_in", proj)
            act.wait_ge(lr_ready, 1)
            act.activation(lr_t, pm[0:RANK, 0, 0:T], ACT.Copy).then_inc(lrt_ready, 1)
            act.wait_ge(z_ready, 1)
            for h in range(HEADS):
                last = act.activation(e_pos[:, h, :], pm[:, h, 0:T], ACT.Abs, bias=pcol("b_gate", h, h + 1))
            last.then_inc(absz_ready, 1)
            act.wait_ge(absz_ready, 1)
            link(act.activation(e_neg, e_pos, ACT.Exp, scale=-1.0))
            act.activation(e_neg, e_neg, ACT.Ln, bias=1.0).then_inc(log_ready, 1)
            act.wait_ge(cum_ready, 1)
            act.activation(e_pos, decay, ACT.Exp, scale=1.0 / TAU).then_inc(exps_ready, 1)
            act.activation(e_neg, decay, ACT.Exp, scale=-1.0 / TAU).then_inc(exps_ready, 1)
            act.wait_ge(dend_ready, 1)
            act.activation(k_end, k_end, ACT.Exp, scale=1.0 / TAU).then_inc(edend_ready, 1)
            for n in range(15):
                c, part = divmod(n, 3)
                rows = CH if c < NCH else 32
                act.wait_ge(tr_ready, n + 1)
                dst = v_tok[0:rows, c, part * 512:part * 512 + 512] if part < 2 else ke_tok[0:rows, c, :]
                act.activation(dst, pm[0:rows, n % 4, :], ACT.Copy).then_inc(tr_evac, 1)
            for c in range(NCH + 1):
                act.wait_ge(o_ready, c + 1)
                cols = slice(c * CH, (c + 1) * CH) if c < NCH else slice(SEQ, T)
                width = 8 * (CH if c < NCH else 32)
                act.activation(ot[:, :, cols], pm[:, 2 + c % 2, 0:width].rearrange("p (a t) -> p a t", a=8),
                               ACT.Copy).then_inc(o_evac, 1)
            act.activation(gt, gt, ACT.Silu).then_inc(silu_ready, 1)
            act.wait_ge(omean_ready, 1)
            act.activation(rms_t, rms_h, ACT.Sqrt).then_inc(oroot_ready, 1)
            act.wait_ge(og_ready, 1)
            act.activation(hid_hi[:], ot, ACT.Copy).then_inc(hh_ready, 1)
            project("gla_out", mix_g)
            norm_root(1)
            peer(0)

            norm_root(2)
            project("rg_in", area(0, 2 * RT, T))
            act.activation(sp[:, 1, :], pcol("lam"), ACT.Abs).then_inc(lame_ready, 1)
            act.wait_ge(lame_ready, 1)
            act.activation(sp[:, 1, :], sp[:, 1, :], ACT.Exp, scale=-1.0).then_inc(lame_ready, 1)
            for gate, (dst, bias) in enumerate(((g_r, "b_a"), (g_i, "b_x"))):
                for o in range(RT):
                    act.wait_ge(gate_used, gate * RT + o + 1)
                    act.activation(dst[:, o, :], pu[:, (gate * RT + o) % 4, 0:T], ACT.Sigmoid,
                                   bias=pcol(bias, o, o + 1)).then_inc(pu_evac, 1)
            act.wait_ge(sp_ready, 1)
            act.wait_ge(pu_evac, BANKED["gates"] + 2 * RT)
            for o in range(RT):
                last = act.activation(av[:, o, :], g_r[:, o, :], ACT.Tanh, scale=sp[:, 7, o:o + 1])
            last.then_inc(tanh_ready, 1)
            act.wait_ge(tanh_ready, 1)
            act.activation(mult, av, ACT.Sqrt).then_inc(sqrt_ready, 1)
            act.activation(yb, yb, ACT.Gelu_apprx_tanh).then_inc(gelu_y, 1)
            act.wait_ge(hg_ready, 1)
            act.activation(hid_hi[:], yb[:, 0:KD, :], ACT.Copy).then_inc(hh_ready, 1)
            project("rg_out", mix_r)
            norm_root(3)
            peer(1)
            norm_root(4)

        @block.tensor
        def _(pe):
            mm = pe.matmul

            def three(out, cols, kk, r_hi, r_lo, s2, n_k, stop=True):
                mm(out, w_hi[:, s2, cols], r_hi, start=(kk == 0), stop=False)
                mm(out, w_hi[:, s2, cols], r_lo, start=False, stop=False)
                return mm(out, w_lo[:, s2, cols], r_hi, start=False, stop=(stop and kk == n_k - 1))

            def chunk(out, s2):
                for kk in range(KD):
                    last = three(out, slice(kk * P, kk * P + P), kk, hid_hi[:, kk, :], hid_lo[:, kk, :], s2, KD)
                return last

            def squares(n):
                pe.wait_ge(sq_ready, n + 1)
                for kk in range(KD):
                    last = mm(pm[:, 0, 0:T], ones[:], hid[:, kk, :], start=(kk == 0), stop=(kk == KD - 1))
                last.then_inc(sum_ready, 1)

            def ada_mm(lay, first_tile, last_tile):
                name = f"ada{lay}"
                full0, u0 = (STREAM[name] // RING + 1) * 16, BANKED[name]

                def group(i, first):
                    for s in range(4):
                        pe.wait_ge(raw_full[s], i * 16 + full0)
                        if u0 or not first:
                            pe.wait_ge(pu_evac, i * 4 + (u0 + s - 3))
                        for kk in range(KD):
                            last = mm(pu[:, s, 0:NSEQ], raw[:, s, kk * P:kk * P + P], cond[:, kk, :],
                                      start=(kk == 0), stop=(kk == KD - 1))
                        last.then_inc(raw_used, 1)

                if first_tile == 0:
                    group(0, True)
                with pe.Fori(max(first_tile // 4, 1), last_tile // 4) as i:
                    group(i, False)

            def project(name):
                m0, u0 = SPLIT[name], BANKED[name]
                pe.wait_ge(hh_ready, MOVING[name])
                pe.wait_ge(hl_ready, MOVING[name])

                def group(i):
                    for s in range(4):
                        pe.wait_ge(lo_done, i * 4 + (m0 + s + 1))
                        pe.wait_ge(pu_evac, i * 4 + (u0 + s - 3))
                        chunk(pu[:, s, 0:T], s % 2).then_inc(split_used, 1)

                with pe.Fori(0, counts[name] // 4) as i:
                    group(i)

            def peer(lay):
                squares(1 + 2 * lay)
                project(f"wq{lay}")
                pe.wait_ge(key_in, 16 * (lay + 1))
                pe.wait_ge(pu_evac, BANKED[f"wq{lay}"] + 16)
                for tt in range(3):
                    rows = P if tt < 2 else 32
                    for b in range(4):
                        if tt:
                            pe.wait_ge(s_evac, lay * 12 + tt * 4 + b - 3)
                        for a in range(4):
                            hp = 4 * b + a
                            last = mm(pm[0:rows, b, a * P:a * P + P], qp[:, hp, tt * P:tt * P + rows], key[:, hp, :],
                                      start=True, stop=True)
                        last.then_inc(s_ready, 1)
                pe.wait_ge(s_evac, lay * 12 + 12)
                for tt in range(3):
                    rows = P if tt < 2 else 32
                    if lay == 0:
                        ada_mm(1, tt * 16, tt * 16 + 16)
                    pe.wait_ge(slot_ready, lay * 3 + tt + 1)
                    for a in range(3):
                        last = pe.transpose(pm[:, tt, a * P:a * P + rows], slot[0:rows, a, :], ident[0:rows, 0:rows])
                    last.then_inc(slot_t, 1)

                name = f"uv{lay}"
                m0, n0, u0 = SPLIT[name], lay * NKEY, BANKED[name]

                def build_g(hf):
                    o0 = (lay * 2 + hf) * (T // 4)
                    e0 = (lay * 2 + hf) * (T // 8)

                    def sixteen(i, first):
                        for b in range(2):
                            if e0 or not first:
                                pe.wait_ge(g_evac, i * 2 + (e0 + b - 1))
                            for h in range(2):
                                pe.wait_ge(oh_ready, i * 4 + (o0 + b * 2 + h + 1))
                                for t in range(4):
                                    last = mm(pg[:, b, (h * 4 + t) * HALF:(h * 4 + t + 1) * HALF], oh_b[:, h, t, :],
                                              oh_a[:, h, t, :], start=True, stop=True)
                                last.then_inc(oh_used, 1)

                    sixteen(0, True)
                    with pe.Fori(1, T // 16) as i:
                        sixteen(i, False)

                def times_v(vo, m, j, s2, group, par, n_w):
                    pe.wait_ge(lo_done, m + 1)
                    if j == 0:
                        pe.wait_ge(w_ready, n_w)
                    if not isinstance(vo, int) or vo >= 2:
                        pe.wait_ge(pv_evac, vo - 1)
                    for jj in range(GRP):
                        last = three(pv[:, j % 2, 0:T], slice(jj * P, jj * P + P), jj, wgt_hi[:, par, jj, :],
                                     wgt_lo[:, par, jj, :], s2, GRP)
                    last.then_inc(split_used, 1)

                def pair_group(g, par):
                    for j in range(GRP):
                        m = g * 16 + (m0 + GRP - 16 + 2 * j)
                        pe.wait_ge(lo_done, m + 1)
                        pe.wait_ge(pu_evac, g * 8 + (u0 + j - 3))
                        chunk(pu[:, j % 4, 0:T], 0).then_inc(split_used, 1)
                        times_v(g * 8 + (n0 - 8 + j), m + 1, j, 1, g - 1, 1 - par, g * 8 + n0)

                build_g(0)
                for j in range(GRP):
                    pe.wait_ge(lo_done, m0 + j + 1)
                    pe.wait_ge(pu_evac, u0 + j - 3)
                    chunk(pu[:, j % 4, 0:T], j % 2).then_inc(split_used, 1)
                pair_group(1, 1)
                with pe.Fori(1, 4) as i:
                    pair_group(i * 2, 0)
                    pair_group(i * 2 + 1, 1)
                build_g(1)
                with pe.Fori(4, 8) as i:
                    pair_group(i * 2, 0)
                    pair_group(i * 2 + 1, 1)
                for j in range(GRP):
                    times_v(n0 + 120 + j, m0 + 248 + j, j, j % 2, 15, 1, n0 + NKEY)

            pe.wait_ge(cond_ready, 1)
            ada_mm(0, 0, 48)
            pe.wait_ge(ones_set, 1)
            squares(0)
            project("gla_in")
            pe.wait_ge(side_in, 32)
            for kk in range(KD):
                last = mm(pm[0:RANK, 0, 0:T], lr_w[:, kk, :], hid[:, kk, :], start=(kk == 0), stop=(kk == KD - 1))
            last.then_inc(lr_ready, 1)
            pe.wait_ge(lrt_ready, 1)
            for h in range(HEADS):
                last = mm(pm[:, h, 0:T], gate2[:, h * P:h * P + P], lr_t, start=True, stop=True)
            last.then_inc(z_ready, 1)
            pe.wait_ge(pu_evac, BANKED["gla_in"] + 24)
            pe.wait_ge(minz_ready, 1)
            pe.wait_ge(absz_ready, 1)
            for n in range(15):
                c, part = divmod(n, 3)
                rows = CH if c < NCH else 32
                if part == 2 and c == 0:
                    pe.wait_ge(ke_ready, 1)
                if n >= 4:
                    pe.wait_ge(tr_evac, n - 3)
                for a in range(4):
                    src = vt[:, part * 4 + a, c * CH:c * CH + rows] if part < 2 else k_end[:, a, c * CH:c * CH + rows]
                    last = pe.transpose(pm[0:rows, n % 4, a * P:a * P + P], src, ident)
                last.then_inc(tr_ready, 1)
            pe.wait_ge(qk_ready, 1)
            pe.wait_ge(tr_evac, 15)
            for c in range(NCH):
                for h in range(HEADS):
                    last = mm(pm[0:CH, c // 2, ((c % 2) * 4 + h) * CH:((c % 2) * 4 + h + 1) * CH],
                              k[:, h, c * CH:(c + 1) * CH], q[:, h, c * CH:(c + 1) * CH], start=True, stop=True)
            for h in range(HEADS):
                last = mm(pu[0:32, 3, h * 32:h * 32 + 32], k[:, h, SEQ:T], q[:, h, SEQ:T], start=True, stop=True)
            last.then_inc(sc_ready, 1)
            pe.wait_ge(sc_masked, 2)
            for c in range(NCH):
                if c >= 2:
                    pe.wait_ge(o_evac, c - 1)
                for a in range(8):
                    last = mm(pm[:, 2 + c % 2, a * CH:(a + 1) * CH], v_tok[0:CH, c, a * P:a * P + P],
                              sc[:, c * 4 + a // 2, :], start=(a == 0), stop=(c == 0 and a == 7), skip_group_check=True)
                if c:
                    pe.wait_ge(s_new, HEADS * c)
                    for a in range(8):
                        last = mm(pm[:, 2 + c % 2, a * CH:(a + 1) * CH], s_pr[:, a // 2, (a % 2) * P:(a % 2) * P + P],
                                  q[:, a // 2, c * CH:(c + 1) * CH], start=False, stop=(a == 7), skip_group_check=True)
                last.then_inc(o_ready, 1)
                for h in range(HEADS):
                    last = mm(pu[:, h // 2, (h % 2) * HDV:(h % 2 + 1) * HDV], ke_tok[0:CH, c, h * P:h * P + P],
                              v_tok[0:CH, c, h * HDV:(h + 1) * HDV], start=True, stop=True)
                last.then_inc(ds_ready, 1)
            for a in range(8):
                if a == 0:
                    pe.wait_ge(o_evac, 3)
                mm(pm[:, 2, a * 32:a * 32 + 32], v_tok[0:32, NCH, a * P:a * P + P], sc_s[:, a // 2, :],
                   start=(a == 0), stop=False, skip_group_check=True)
            pe.wait_ge(s_new, HEADS * NCH)
            for b in range(NB):
                pe.wait_ge(st_in[b % 2], 16 * (b // 2 + 1))
                for a in range(8):
                    last = mm(pm[:, 2, a * 32 + b * NT:a * 32 + b * NT + NT],
                              s_in[:, b % 2, a * P:a * P + P], q[:, a // 2, SEQ + b * NT:SEQ + b * NT + NT],
                              start=False, stop=(b == NB - 1 and a == 7), skip_group_check=True)
                if b == NB - 1:
                    last.then_inc(o_ready, 1)
                pe.wait_ge(kem_ready, b + 1)
                if b >= 2:
                    pe.wait_ge(stn_ready, HEADS * (b - 1))
                for h in range(HEADS):
                    last = mm(pu[:, (b % 2) * 2 + h // 2, (h % 2) * HDV:(h % 2 + 1) * HDV],
                              ke_m[:, b % 2, h * P:h * P + P], v_tok[0:32, NCH, h * HDV:(h + 1) * HDV],
                              start=True, stop=True)
                last.then_inc(st_used, 1)
            pe.wait_ge(osq_ready, 1)
            for h in range(HEADS):
                for e in range(2):
                    last = mm(pm[:, h, 0:T], ones[:], hid[:, 2 * h + e, :], start=(e == 0), stop=(e == 1))
            last.then_inc(osum_ready, 1)
            project("gla_out")
            peer(0)

            squares(2)
            project("rg_in")
            pe.wait_ge(conv_ready, 1)
            for c in range(8):
                gate, sg, part = c // 4, c // 2 % 2, c % 2
                pe.wait_ge(raw_full[c % 4], (STREAM["gates"] // RING + 1 + c // 4) * 16)
                pairs = GATE_PAIRS[part]
                for n, (src, dst) in enumerate(pairs):
                    o = gate * RT + sg * 5 + dst
                    first = n == 0 or pairs[n - 1][1] != dst
                    done = n == len(pairs) - 1 or pairs[n + 1][1] != dst
                    if first:
                        pe.wait_ge(pu_evac, BANKED["gates"] + o - 3)
                    last = mm(pu[:, o % 4, 0:T], raw[:, c % 4, n * P:n * P + P], xc[:, sg * 5 + src, :],
                              start=first, stop=done)
                    if done:
                        last.then_inc(gate_used, 1)
            pe.wait_ge(hh_ready, MOVING["rg_out"])
            pe.wait_ge(hl_ready, MOVING["rg_out"])
            pe.wait_ge(rg_side, 48)
            for o in range(KD):
                pe.wait_ge(lo_done, SPLIT["rg_out"] + o + 1)
                pe.wait_ge(pu_evac, BANKED["rg_out"] + o - 3)
                for e in range(2):
                    mm(pu[:, o % 4, 0:T], tail[:, e, o * P:o * P + P], yb[:, KD + e, :], start=(e == 0), stop=False)
                for kk in range(KD):
                    last = three(pu[:, o % 4, 0:T], slice(kk * P, kk * P + P), kk + 1, hid_hi[:, kk, :],
                                 hid_lo[:, kk, :], o % 2, KD + 1)
                last.then_inc(split_used, 1)
            peer(1)
            squares(4)

        @block.vector
        def _(dve):
            own = [0]
            tt_, ts, stt = dve.tensor_tensor, dve.tensor_scalar, dve.scalar_tensor_tensor

            def link(ins):
                own[0] += 1
                ins.then_inc(vec, 1)
                dve.wait_ge(vec, own[0])

            def bc(v, *shape):
                for axis in range(len(v.shape), len(shape)):
                    v = v.unsqueeze(axis)
                return v.to_broadcast(list(shape))

            def samples(v):
                return v[:, :, SEQ:T].rearrange("p k (b t) -> p k b t", b=NB)

            def low(m, s4, s2):
                dve.wait_ge(hi_done, m + 1)
                tt_(w_lo[:, s2, :], raw[:, s4, :], w_hi[:, s2, :].bitcast(F32), ALU.subtract).then_inc(lo_done, 1)

            def lows(name):
                with dve.Fori(0, counts[name] // 4) as i:
                    for s in range(4):
                        low(i * 4 + (SPLIT[name] + s), s, s % 2)

            def moving_low(src, n):
                dve.wait_ge(hh_ready, n)
                tt_(hid_lo[:], src, hid_hi[:].bitcast(F32), ALU.subtract).then_inc(hl_ready, 1)

            def norm(n, gain, lay=0, j_shift=0):
                tt_(hid[:], x[:], x[:], ALU.mult).then_inc(sq_ready, 1)
                if n < 4:
                    link(stt(coef[:], mod[:, lay, j_shift + 1], 1.0, bc(gain, P, KD, NSEQ), ALU.add, ALU.mult))
                dve.wait_ge(sum_ready, n + 1)
                ts(mean[:], pm[:, 0, 0:T], 1.0 / D, EPS, ALU.mult, ALU.add).then_inc(mean_ready, 1)
                dve.wait_ge(mean_ready, n + 1)
                dve.wait_ge(root_ready, n + 1)
                inverse_root(root[:], mean[:], newt[:])
                link(tt_(hid[:], x[:], root[:].unsqueeze(1).to_broadcast([P, KD, T]), ALU.mult))
                if n == 4:
                    tt_(hid[:], hid[:], bc(gain, P, KD, T), ALU.mult).then_inc(out_ready, 1)
                    return
                for kk in range(KD):
                    last = ts(hid[:, kk, 0:SEQ], hid[:, kk, 0:SEQ], coef[:, kk, 0:1], mod[:, lay, j_shift, kk, 0:1],
                              ALU.mult, ALU.add)
                link(tt_(samples(hid[:]), samples(hid[:]), bc(coef[:, :, 1:NSEQ], P, KD, NB, NT), ALU.mult))
                tt_(samples(hid[:]), samples(hid[:]), bc(mod[:, lay, j_shift, :, 1:NSEQ], P, KD, NB, NT),
                    ALU.add).then_inc(hid_ready, 1)
                dve.wait_ge(hid_ready, n + 1)
                moving_low(hid[:], {0: 1, 1: 3, 2: 4, 3: 6}[n])

            def inverse_root(r, m, t):
                link(dve.reciprocal(r, r))
                link(tt_(t, r, r, ALU.mult))
                link(tt_(t, t, m, ALU.mult))
                link(ts(t, t, -0.5, 1.5, ALU.mult, ALU.add))
                link(tt_(r, r, t, ALU.mult))

            def residual(src, lay, j_gate):
                for kk in range(KD):
                    stt(x[:, kk, 0:SEQ], src[:, kk, 0:SEQ], mod[:, lay, j_gate, kk, 0:1], x[:, kk, 0:SEQ],
                        ALU.mult, ALU.add)
                link(tt_(samples(src), samples(src), bc(mod[:, lay, j_gate, :, 1:NSEQ], P, KD, NB, NT), ALU.mult))
                link(tt_(samples(x[:]), samples(x[:]), samples(src), ALU.add))

            def top16(rows, values, n, width, out, out_i):
                for part in range(2):
                    at = slice(part * 8, part * 8 + 8)
                    for a in range(n):
                        last = dve.max(out[0:rows, a, at], values[0:rows, a, 0:width])
                    link(last)
                    for a in range(n):
                        last = dve.max_index(out_i[0:rows, a, at], out[0:rows, a, at], values[0:rows, a, 0:width])
                    if part == 0:
                        for a in range(n):
                            last = dve.match_replace(values[0:rows, a, 0:width], out[0:rows, a, at],
                                                     values[0:rows, a, 0:width], LOWEST)
                    link(last)

            def route(lay, tt):
                rows = P if tt < 2 else 32
                if tt:
                    dve.wait_ge(slot_t, lay * 3 + tt)
                dve.wait_ge(s_evac, lay * 12 + tt * 4 + 4)
                top16(rows, scor[:, tt], 16, NKEY, val, idx)
                dve.tensor_copy(idx_f[0:rows], idx[0:rows])
                pair = val[0:rows].rearrange("p (h two) a -> p h two a", two=2)
                for h in range(PH):
                    last = tt_(cand[0:rows, h, :].rearrange("p (a b) -> p a b", a=TOPK),
                               bc(pair[:, h, 0, :], rows, TOPK, TOPK),
                               pair[:, h, 1, :].unsqueeze(1).to_broadcast([rows, TOPK, TOPK]), ALU.add)
                link(last)
                top16(rows, cand, PH, 256, best, pos)
                tt_(slot[0:rows, 2, :].rearrange("p (h a) -> p h a", h=PH), best[0:rows],
                    best[0:rows, :, 0:1].to_broadcast([rows, PH, TOPK]), ALU.subtract).then_inc(shift_ready, 1)
                flat = pos[0:rows].rearrange("p h a -> p (h a)")
                ts(pa[0:rows], flat, 4, None, ALU.logical_shift_right)
                link(ts(pb[0:rows], flat, 15, None, ALU.bitwise_and))
                dve.tensor_copy(pa_f[0:rows], pa[0:rows])
                link(dve.tensor_copy(pb_f[0:rows], pb[0:rows]))
                place = iota[0:rows, 0:TOPK].unsqueeze(1).to_broadcast([rows, SLOTS, TOPK])
                pair_i = idx_f[0:rows].rearrange("p (h two) a -> p h two a", two=2)
                for which, src in enumerate((pa_f, pb_f)):
                    link(tt_(onek[0:rows], bc(src[0:rows], rows, SLOTS, TOPK), place, ALU.is_equal))
                    for h in range(PH):
                        rng = onek[0:rows, h * TOPK:(h + 1) * TOPK, :]
                        last = tt_(rng, rng, pair_i[:, h, which, :].unsqueeze(1).to_broadcast([rows, TOPK, TOPK]), ALU.mult)
                    link(last)
                    link(dve.tensor_reduce(slot[0:rows, which, :], onek[0:rows], AX_X, ALU.add))
                dve.wait_ge(exp_ready, lay * 3 + tt + 1)
                wv = slot[0:rows, 2, :].rearrange("p (h a) -> p h a", h=PH)
                link(dve.tensor_reduce(ssum[0:rows, 0, :], wv, AX_X, ALU.add))
                link(dve.reciprocal(ssum[0:rows, 1, :], ssum[0:rows, 0, :]))
                tt_(wv, wv, bc(ssum[0:rows, 1, :], rows, PH, TOPK), ALU.mult).then_inc(slot_ready, 1)

            def peer(lay):
                norm(1 + 2 * lay, pcol("ffn_g", lay * KD, lay * KD + KD), lay, 3)
                lows(f"wq{lay}")
                link(dve.memset(hid[:], 0.0))
                for tt in range(3):
                    route(lay, tt)
                for tt in range(3):
                    rows = P if tt < 2 else 32
                    dve.wait_ge(slot_t, lay * 3 + tt + 1)
                    last = dve.tensor_copy(sel[:, :, tt * P:tt * P + rows],
                                           pm[:, tt, 0:384].rearrange("p (a t) -> p a t", a=3)[:, :, 0:rows])
                link(last)
                name = f"uv{lay}"
                m0, n0, u0 = SPLIT[name], lay * NKEY, BANKED[name]

                def one_hots(hf):
                    o0 = (lay * 2 + hf) * (T // 4)

                    def eight(i, first):
                        for h in range(2):
                            if o0 or not first:
                                dve.wait_ge(oh_used, i * 2 + (o0 + h - 1))
                            for t in range(4):
                                tok = bass.ds(i * 8 + (h * 4 + t), 1)
                                ts(oh_b[:, h, t, :], iota, sel[:, 1, tok], sel[:, 2, tok], ALU.is_equal, ALU.mult)
                                last = ts(oh_a[:, h, t, :], iota[:, hf * HALF:(hf + 1) * HALF], sel[:, 0, tok], None,
                                          ALU.is_equal)
                            last.then_inc(oh_ready, 1)

                    eight(0, True)
                    with dve.Fori(1, T // 8) as i:
                        eight(i, False)
                    dve.wait_ge(g_evac, (lay * 2 + hf + 1) * (T // 8))

                def weigh(n, gi, buf, par, j):
                    dve.wait_ge(pu_evac, n + (u0 - n0 + 1))
                    row = g_mat[:, bass.ds(gi, 1), :].rearrange("p a t -> p (a t)")
                    if not isinstance(n, int) or n:
                        dve.wait_ge(w_ready, n)
                    tt_(wgt[:], gel[:, buf, :], row, ALU.mult).then_inc(gel_used, 1)
                    dve.wait_ge(gel_used, n + 1)
                    dve.tensor_copy(wgt_hi[:, par, j, :], wgt[:]).then_inc(wh_ready, 1)
                    dve.wait_ge(wh_ready, n + 1)
                    tt_(wgt_lo[:, par, j, :], wgt[:], wgt_hi[:, par, j, :].bitcast(F32), ALU.subtract).then_inc(w_ready, 1)

                def add_v(vo, m, j):
                    dve.wait_ge(split_used, m + 1)
                    tt_(hid[:, j, :], hid[:, j, :], pv[:, j % 2, 0:T], ALU.add).then_inc(pv_evac, 1)

                def pair_group(g, par, g_half, add_before=True):
                    for j in range(GRP):
                        m = g * 16 + (m0 + GRP - 16 + 2 * j)
                        low(m, (2 * j) % 4, 0)
                        if j:
                            weigh(g * 8 + (n0 + j - 1), g * 8 + (j - 1 - g_half * HALF), (j - 1) % 2, par, j - 1)
                        low(m + 1, (2 * j + 1) % 4, 1)
                        if j or add_before:
                            add_v(g * 8 + (n0 - 8 + j - 1), m - 1, (j - 1) % GRP)
                    weigh(g * 8 + (n0 + GRP - 1), g * 8 + (GRP - 1 - g_half * HALF), 1, par, GRP - 1)

                one_hots(0)
                for j in range(GRP):
                    low(m0 + j, j % 4, j % 2)
                    if j:
                        weigh(n0 + j - 1, j - 1, (j - 1) % 2, 0, j - 1)
                weigh(n0 + GRP - 1, GRP - 1, 1, 0, GRP - 1)
                pair_group(1, 1, 0, add_before=False)
                with dve.Fori(1, 4) as i:
                    pair_group(i * 2, 0, 0)
                    pair_group(i * 2 + 1, 1, 0)
                one_hots(1)
                with dve.Fori(4, 8) as i:
                    pair_group(i * 2, 0, 1)
                    pair_group(i * 2 + 1, 1, 1)
                for j in range(GRP):
                    low(m0 + 248 + j, j % 4, j % 2)
                    add_v(n0 + 120 + j - 1, m0 + 248 + j - 1, (j - 1) % GRP)
                add_v(n0 + 127, m0 + 255, GRP - 1)
                dve.wait_ge(pv_evac, n0 + NKEY)
                residual(hid[:], lay, 5)

            dve.wait_ge(consts_in, 64)
            dve.wait_ge(pu_evac, 48)
            norm(0, pcol("mix_g", 0, KD), 0, 0)
            lows("gla_in")
            dve.wait_ge(absz_ready, 1)
            for h in range(HEADS):
                last = ts(decay[:, h, :], pm[:, h, 0:T], pcol("b_gate", h, h + 1), 0.0, ALU.add, ALU.min)
            last.then_inc(minz_ready, 1)
            dve.wait_ge(minz_ready, 1)
            dve.wait_ge(log_ready, 1)
            link(tt_(decay, decay, e_neg, ALU.subtract))
            for h in range(HEADS):
                last = dve.tensor_tensor_scan(decay[:, h, :], ccol("keep"), decay[:, h, :], 0.0, ALU.mult, ALU.add)
            last.then_inc(cum_ready, 1)
            dve.wait_ge(cum_ready, 1)
            for h in range(HEADS):
                b4 = decay[:, h, 0:SEQ].rearrange("p (c t) -> p c t", c=NCH)
                tt_(k_end[:, h, 0:SEQ].rearrange("p (c t) -> p c t", c=NCH),
                    b4[:, :, CH - 1:CH].to_broadcast([P, NCH, CH]), b4, ALU.subtract)
                s4 = decay[:, h, SEQ:T].rearrange("p (b t) -> p b t", b=NB)
                last = tt_(k_end[:, h, SEQ:T].rearrange("p (b t) -> p b t", b=NB),
                           s4[:, :, NT - 1:NT].to_broadcast([P, NB, NT]), s4, ALU.subtract)
            last.then_inc(dend_ready, 1)
            dve.wait_ge(edend_ready, 1)
            dve.wait_ge(pu_evac, BANKED["gla_in"] + 24)
            tt_(k_end, k_end, k, ALU.mult).then_inc(ke_ready, 1)
            dve.wait_ge(exps_ready, 2)
            stt(q, q, float(P) ** -0.5, e_pos, ALU.mult, ALU.mult)
            tt_(k, k, e_neg, ALU.mult).then_inc(qk_ready, 1)
            dve.wait_ge(sc_ready, 1)
            for c2 in range(2):
                tt_(sc[:, c2 * 8:c2 * 8 + 8, :], pm[0:CH, c2, :].rearrange("p (a t) -> p a t", a=8),
                    ccol("causal", CH).unsqueeze(1).to_broadcast([CH, 8, CH]), ALU.mult).then_inc(sc_masked, 1)
            tt_(sc_s, pu[0:32, 3, 0:P].rearrange("p (a t) -> p a t", a=HEADS),
                ccol("sample_causal", 32).unsqueeze(1).to_broadcast([32, HEADS, 32]), ALU.mult).then_inc(sc_masked, 1)
            for c in range(NCH):
                dve.wait_ge(ds_ready, c + 1)
                if c:
                    dve.wait_ge(o_ready, c + 1)
                    dve.wait_ge(s_new, HEADS * c)
                for h in range(HEADS):
                    add = pu[:, h // 2, (h % 2) * HDV:(h % 2 + 1) * HDV]
                    end = c * CH + CH - 1
                    if c == 0:
                        dve.tensor_copy(s_pr[:, h, :], add).then_inc(s_new, 1)
                    else:
                        stt(s_pr[:, h, :], s_pr[:, h, :], e_pos[:, h, end:end + 1], add, ALU.mult, ALU.add).then_inc(s_new, 1)
            for b in range(NB):
                if b >= 2:
                    dve.wait_ge(st_used, b - 1)
                ts(ke_m[:, b % 2, :], ke_tok[0:32, NCH, :], ccol("seq_mask", 32)[:, b:b + 1], None,
                   ALU.mult).then_inc(kem_ready, 1)
                dve.wait_ge(st_used, b + 1)
                for h in range(HEADS):
                    s_v = s_in[:, b % 2, h * HDV:(h + 1) * HDV]
                    end = SEQ + b * NT + NT - 1
                    stt(s_v, s_v, e_pos[:, h, end:end + 1],
                        pu[:, (b % 2) * 2 + h // 2, (h % 2) * HDV:(h % 2 + 1) * HDV], ALU.mult,
                        ALU.add).then_inc(stn_ready, 1)
            dve.wait_ge(o_evac, NCH + 1)
            tt_(hid[:], ot, ot, ALU.mult).then_inc(osq_ready, 1)
            dve.wait_ge(osum_ready, 1)
            ts(rms_h, pm[:, :, 0:T], 1.0 / HDV, EPS, ALU.mult, ALU.add).then_inc(omean_ready, 1)
            dve.wait_ge(omean_ready, 1)
            dve.wait_ge(oroot_ready, 1)
            inverse_root(rms_t, rms_h, decay)
            heads = ot.rearrange("p (h e) t -> p h e t", e=2)
            for e in range(2):
                last = stt(heads[:, :, e, :], heads[:, :, e, :], pcol("onorm_g", e, e + 1), rms_t, ALU.mult, ALU.mult)
            link(last)
            dve.wait_ge(silu_ready, 1)
            tt_(ot, ot, gt, ALU.mult).then_inc(og_ready, 1)
            dve.wait_ge(og_ready, 1)
            moving_low(ot, 2)
            lows("gla_out")
            dve.wait_ge(pu_evac, BANKED["gla_out"] + 8)
            residual(mix_g, 0, 2)
            peer(0)

            norm(2, pcol("mix_g", KD, 2 * KD), 1, 0)
            lows("rg_in")
            dve.wait_ge(pu_evac, BANKED["rg_in"] + 20)
            dve.wait_ge(rg_side, 48)
            cw = pcol("conv_w")
            for o in range(RT):
                last = ts(xc[:, o, :], xb[:, o, :], cw[:, 3 * RT + o:3 * RT + o + 1], pcol("conv_b", o, o + 1),
                          ALU.mult, ALU.add)
            dve.tensor_copy(xs[:, :, :, 0:3], conv0)
            link(dve.tensor_copy(xs[:, :, :, 3:7], samples(xb)))
            for tap in range(3):
                back = 3 - tap
                for o in range(RT):
                    last = stt(xc[:, o, back:SEQ], xb[:, o, 0:SEQ - back], cw[:, tap * RT + o:tap * RT + o + 1],
                               xc[:, o, back:SEQ], ALU.mult, ALU.add)
                link(tt_(tmp_s, xs[:, :, :, tap:tap + 4], bc(cw[:, tap * RT:(tap + 1) * RT], P, RT, NB, NT), ALU.mult))
                link(tt_(samples(xc), samples(xc), tmp_s, ALU.add))
            dve.tensor_copy(cs_out, xs[:, :, :, 4:7])
            dve.tensor_copy(cp_out, xb[:, :, SEQ - 3:SEQ]).then_inc(conv_ready, 1)
            dve.wait_ge(lame_ready, 2)
            link(ts(sp[:, 2, :], sp[:, 1, :], 2.0, None, ALU.add))
            link(dve.reciprocal(sp[:, 2, :], sp[:, 2, :]))
            link(tt_(sp[:, 3, :], sp[:, 1, :], sp[:, 2, :], ALU.mult))
            link(tt_(sp[:, 4, :], sp[:, 3, :], sp[:, 3, :], ALU.mult))
            link(ts(sp[:, 5, :], sp[:, 4, :], 1.0 / 17, 1.0 / 15, ALU.mult, ALU.add))
            for odd in (13, 11, 9, 7, 5, 3, 1):
                link(tt_(sp[:, 5, :], sp[:, 5, :], sp[:, 4, :], ALU.mult))
                link(ts(sp[:, 5, :], sp[:, 5, :], 1.0 / odd, None, ALU.add))
            link(tt_(sp[:, 5, :], sp[:, 5, :], sp[:, 3, :], ALU.mult))
            link(ts(sp[:, 6, :], pcol("lam"), -4.0, 0.0, ALU.mult, ALU.max))
            stt(sp[:, 7, :], sp[:, 5, :], 8.0, sp[:, 6, :], ALU.mult, ALU.add).then_inc(sp_ready, 1)
            dve.wait_ge(tanh_ready, 1)
            link(ts(g_r, av, -1.0, -1.0, ALU.mult, ALU.add))
            link(dve.reciprocal(g_r, g_r))
            dve.wait_ge(sqrt_ready, 1)
            stt(av, av, 1.0, g_r, ALU.subtract, ALU.mult)
            link(stt(mult, mult, -2.0, g_r, ALU.mult, ALU.mult))
            dve.memset(av[:, :, 0:1], 0.0)
            link(dve.memset(mult[:, :, 0:1], 1.0))
            link(tt_(mult, mult, g_i, ALU.mult))
            link(tt_(mult, mult, xc, ALU.mult))
            a0, b0 = samples(av)[:, :, :, 0], samples(mult)[:, :, :, 0]
            link(tt_(h0, a0, h0, ALU.mult))
            link(tt_(b0, b0, h0, ALU.add))
            link(dve.memset(a0, 0.0))
            link(dve.tensor_tensor_scan(g_r.rearrange("p a t -> p (a t)"), av.rearrange("p a t -> p (a t)"),
                                        mult.rearrange("p a t -> p (a t)"), 0.0, ALU.mult, ALU.add))
            dve.tensor_copy(hl_out[:, :, 0:1], g_r[:, :, SEQ - 1:SEQ])
            dve.tensor_copy(hl_out[:, :, 1:NSEQ], samples(g_r)[:, :, :, NT - 1]).then_inc(hs_ready, 1)
            dve.wait_ge(gelu_y, 1)
            tt_(yb, yb, g_r, ALU.mult).then_inc(hg_ready, 1)
            dve.wait_ge(hg_ready, 1)
            moving_low(yb[:, 0:KD, :], 5)
            lows("rg_out")
            dve.wait_ge(pu_evac, BANKED["rg_out"] + 8)
            residual(mix_r, 1, 2)
            peer(1)
            norm(4, pcol("final_g"))


_PARAMS = ["xt", "ct", "par", "con", "ada", "gla_in", "w_lr", "w_gate2", "gla_out", "wq", "keys", "u_tab", "v_tab",
           "rg_in", "gates", "rg_out", "rg_tail", "gla_state", "h_state", "conv_state"]
_OUTS = [("y", (P, KD, T)), ("gla_p", (P, HEADS, HDV)), ("gla_s", (NB, P, D)), ("h", (P, RT, NSEQ)),
         ("conv_p", (P, RT, 3)), ("conv_s", (P, RT, NB, 3))]


def kernel(**inputs):
    import numpy as np
    import concourse.bacc as bacc
    from concourse.bass_utils import run_bass_kernel_spmd

    w = {n: np.asarray(a) for n, a in inputs.items()}

    def chunks(a):
        kk, n = a.shape[0] // P, a.shape[1] // P
        return a.reshape(kk, P, n, P).transpose(2, 1, 0, 3).reshape(n, P, kk * P)

    def cols(a):
        return a.reshape(-1, P).T

    tokens = np.concatenate([w["x_prompt"].reshape(SEQ, D), w["x_sample"].reshape(NB * NT, D)])
    cond = np.concatenate([w["c_prompt"], w["c_sample"]])
    parts = {"ada_b": w["ada_b"], "mix_g": w["norm_mix_g"], "ffn_g": w["norm_ffn_g"], "final_g": w["final_norm_g"],
             "b_gate": w["gla_b_gate"], "onorm_g": w["gla_onorm_g"], "lam": w["rg_lambda"], "b_a": w["rg_b_a"],
             "b_x": w["rg_b_x"], "conv_w": w["rg_conv_w"], "conv_b": w["rg_conv_b"]}
    seq_of = np.arange(NB * NT) // NT
    keep = np.ones(T, np.float32)
    keep[0:SEQ:CH] = 0
    keep[SEQ::NT] = 0
    con = np.zeros((P, CON_N), np.float32)
    for name, v in (("ident", np.eye(P)), ("iota", np.tile(np.arange(P), (P, 1))), ("keep", np.tile(keep, (P, 1))),
                    ("causal", np.triu(np.ones((CH, CH)))),
                    ("sample_causal", np.triu(np.ones((32, 32))) * (seq_of[:, None] == seq_of[None])),
                    ("seq_mask", seq_of[:, None] == np.arange(NB)[None])):
        con[:v.shape[0], CON_COLS[name][0]:CON_COLS[name][1]] = v
    gates = np.zeros((8, P, 8, P), np.float32)
    for n, name in enumerate(("rg_w_a", "rg_w_x")):
        for sg in range(2):
            dense = np.zeros((640, 640), np.float32)
            for b in range(4):
                dense[b * 160:(b + 1) * 160, b * 160:(b + 1) * 160] = w[name][0, sg * 4 + b]
            for part in range(2):
                for at, (src, dst) in enumerate(GATE_PAIRS[part]):
                    gates[n * 4 + sg * 2 + part, :, at] = dense[src * P:(src + 1) * P, dst * P:(dst + 1) * P]
    main_in = w["gla_w_in"][0][:, :3 * D]
    arrays = {
        "xt": tokens.reshape(T, KD, P).transpose(2, 1, 0),
        "ct": cond.reshape(NSEQ, KD, P).transpose(2, 1, 0),
        "par": np.concatenate([cols(parts[n]) for n in PAR_COLS], axis=1),
        "con": con,
        "ada": np.stack([chunks(w["ada_w"][i]) for i in range(2)]),
        "gla_in": chunks(main_in),
        "w_lr": w["gla_w_in"][0][:, 3 * D:].reshape(KD, P, RANK).transpose(1, 0, 2),
        "w_gate2": w["gla_w_gate2"][0],
        "gla_out": chunks(w["gla_w_out"][0]),
        "wq": np.stack([chunks(w["peer_w_q"][i]) for i in range(2)]),
        "keys": w["peer_sub_keys"].reshape(2, 16, NKEY, P).transpose(0, 3, 1, 2),
        "u_tab": w["peer_u"].reshape(2, NKEY, NKEY, KD, P).transpose(0, 1, 4, 3, 2).reshape(2, NKEY, P, D),
        "v_tab": w["peer_v"].reshape(2, NGRP, GRP, NKEY, KD, P).transpose(0, 1, 4, 3, 2, 5).reshape(2, NKEY, P, D),
        "rg_in": chunks(w["rg_w_in"][0]),
        "gates": gates.reshape(8, P, D),
        "rg_out": chunks(w["rg_w_out"][0][:D]),
        "rg_tail": w["rg_w_out"][0][D:].reshape(2, P, D).transpose(1, 0, 2),
        "gla_state": w["state_gla"][0].transpose(0, 2, 1, 3).reshape(NB, P, D),
        "h_state": w["state_rglru_h"][0].reshape(NB, RT, P).transpose(2, 1, 0),
        "conv_state": w["state_rglru_conv"][0].reshape(NB, 3, RT, P).transpose(3, 2, 0, 1),
    }
    nc = bacc.Bacc("TRN2", target_bir_lowering=False, num_devices=1)
    feed, args = {}, []
    for name in _PARAMS:
        a = np.ascontiguousarray(arrays[name])
        feed[f"in_{name}"] = a
        args.append(nc.dram_tensor(f"in_{name}", a.shape, mybir.dt.from_np(a.dtype), kind="ExternalInput").ap())
    for name, shape in _OUTS:
        args.append(nc.dram_tensor(f"out_{name}", shape, F32, kind="ExternalOutput").ap())
    build_step(nc, *args)
    r = run_bass_kernel_spmd(nc, [feed], core_ids=[0]).results[0]
    y = r["out_y"].transpose(2, 1, 0).reshape(T, D)
    h = r["out_h"].transpose(2, 1, 0).reshape(NSEQ, DR)
    return (y[:SEQ].reshape(1, SEQ, D), y[SEQ:].reshape(NB, NT, D),
            r["out_gla_p"].transpose(1, 0, 2).reshape(1, 1, HEADS, P, HDV),
            r["out_gla_s"].reshape(1, NB, P, HEADS, HDV).transpose(0, 1, 3, 2, 4),
            h[:1].reshape(1, 1, DR), h[1:].reshape(1, NB, DR),
            r["out_conv_p"].transpose(2, 1, 0).reshape(1, 1, 3, DR),
            r["out_conv_s"].transpose(2, 3, 1, 0).reshape(1, NB, 3, DR))
```

```python
from contextlib import ExitStack

import concourse.bass as bass
from concourse import mybir

F32 = mybir.dt.float32
F32R = mybir.dt.float32r
U32 = mybir.dt.uint32
ALU = mybir.AluOpType
ACT = mybir.ActivationFunctionType
AX_X = mybir.AxisListType.X

P = 128
D = 1024
KD = D // P
SEQ = 256
NB, NT = 8, 4
T = SEQ + NB * NT
NSEQ = 1 + NB
EPS = 1e-6
HEADS, HDV = 4, 256
CH = 64
NCH = SEQ // CH
TAU = 16.0
RANK = 16
DR = 1280
RT = DR // P
PH, TOPK, NKEY = 8, 16, 128
SLOTS = PH * TOPK
GRP = 4
HALF = NKEY // 2
ONEK_TILE = HALF - 8
LOWEST = -3.0e38
RING = 4

PAR_COLS = {}
_at = 0
for _name, _n in (("ada_b", 96), ("mix_g", 16), ("ffn_g", 16), ("final_g", 8), ("b_gate", 4), ("onorm_g", 2),
                  ("lam", RT), ("b_a", RT), ("b_x", RT), ("conv_w", 4 * RT), ("conv_b", RT)):
    PAR_COLS[_name] = (_at, _at + _n)
    _at += _n
PAR_N = _at
CON_COLS = {}
_at = 0
for _name, _n in (("ident", 128), ("iota", 128), ("keep", T), ("causal", CH), ("sample_causal", 32), ("seq_mask", NB)):
    CON_COLS[_name] = (_at, _at + _n)
    _at += _n
CON_N = _at

GATE_PAIRS = [[(0, 0), (1, 0), (0, 1), (1, 1), (2, 1), (1, 2), (2, 2), (3, 2)],
              [(2, 3), (3, 3), (4, 3), (3, 4), (4, 4)]]

SEGMENTS = [("ada_a", 16, "raw"), ("gla_in", 24, "split"), ("ada_b", 48, "raw"), ("gla_out", 8, "split"),
            ("wq0", 16, "split"), ("uv0", 256, "split"), ("rg_in", 20, "split"), ("ada_c", 32, "raw"),
            ("gates", 8, "raw"), ("rg_out", 8, "split"), ("wq1", 16, "split"), ("uv1", 256, "split")]
STREAM, SPLIT, LOWS, BANKED, RAW = {}, {}, {}, {}, {}
_n = _m = _l = _u = _r = 0
for _name, _c, _kind in SEGMENTS:
    STREAM[_name], SPLIT[_name], LOWS[_name], BANKED[_name], RAW[_name] = _n, _m, _l, _u, _r
    _n += _c
    _m += _c if _kind == "split" else 0
    _l += (_c - HALF if _name[:2] == "uv" else _c) if _kind == "split" else 0
    _u += 0 if _name[:3] == "ada" else {"uv0": NKEY, "uv1": NKEY, "gates": 2 * RT}.get(_name, _c)
    _r += _c if _name[:3] == "ada" else 0


def build_step(nc, xt, ct, par, con, ada, gla_in, w_lr, w_gate2, gla_out, wq, keys, u_tab, v_tab, rg_in, gates,
               rg_out, rg_tail, gla_state, h_state, conv_state,
               y_out, gla_p_out, gla_s_out, h_out, conv_p_out, conv_s_out):
    with ExitStack() as ctx:
        def sb(name, shape, dt=F32):
            return ctx.enter_context(nc.sbuf_tensor(name, shape, dt))

        def sem(name):
            return ctx.enter_context(nc.semaphore(name))

        x = sb("x", [P, KD, T])
        hid = sb("hid", [P, KD, T])
        hid_hi = sb("hid_hi", [P, KD, T], F32R)
        hid_lo = sb("hid_lo", [P, KD, T], F32R)
        raw = sb("raw", [P, RING, D])
        w_hi = sb("w_hi", [P, 2, D], F32R)
        w_lo = sb("w_lo", [P, 2, D], F32R)
        wgt_hi = sb("wgt_hi", [P, 2, GRP, T], F32R)
        wgt_lo = sb("wgt_lo", [P, 2, GRP, T], F32R)
        mod = sb("mod", [P, 2, 6, KD, NSEQ])
        parm = sb("parm", [P, PAR_N])
        const = sb("const", [P, CON_N])
        cond = sb("cond", [P, KD, NSEQ])
        coef = sb("coef", [P, KD, NSEQ])
        ones = sb("ones", [P, P])
        mean = sb("mean", [P, T])
        root = sb("root", [P, T])
        newt = sb("newt", [P, T])
        arena = sb("arena", [P, 26128])

        def area(at, *dims, dt=F32, parts=P):
            n = 1
            for d in dims:
                n *= d
            v = arena[0:parts, at:at + n]
            if dt != F32:
                v = v.bitcast(dt)
            if len(dims) == 2:
                return v.rearrange("p (a b) -> p a b", a=dims[0])
            if len(dims) == 3:
                return v.rearrange("p (a b c) -> p a b c", a=dims[0], b=dims[1])
            return v

        ada_row = area(21376, D, parts=NSEQ)

        proj = area(0, 24, T)
        q, k = proj[:, 0:4, :], proj[:, 4:8, :]
        vt, gt = proj[:, 8:16, :], proj[:, 16:24, :]
        ot = vt
        mix_g = area(0, KD, T)
        decay = area(6912, HEADS, T)
        e_pos = area(8064, HEADS, T)
        e_neg = area(9216, HEADS, T)
        k_end = area(10368, HEADS, T)
        lr_t = area(10368, T, parts=RANK)
        lr_w = area(18432, KD, RANK)
        gate2 = area(18432 + KD * RANK, 4 * P, parts=RANK)
        v_tok = area(11520, 5, D)
        ke_tok = area(16640, 5, 512)
        sc = area(19200, NCH * HEADS, CH, parts=CH)
        sc_s = area(20224, HEADS, 32, parts=32)
        s_pr = area(20352, HEADS, HDV)
        ke_m = area(6912, 2, 512, parts=32)
        s_in = area(9216, 2, D)
        rms_h = area(0, HEADS, T)
        rms_t = area(1152, HEADS, T)
        yb = area(0, RT, T)
        xb = area(2880, RT, T)
        xc = area(5760, RT, T)
        g_r = area(8640, RT, T)
        g_i = area(11520, RT, T)
        av = area(14400, RT, T)
        mult = xb
        xs = area(17280, RT, NB, 7)
        h0 = area(17840, RT, NB)
        conv0 = area(17920, RT, NB, 3)
        tail = area(18160, 2, D)
        sp = area(20208, 8, RT)
        tmp_s = area(20320, RT, NB, NT)
        hl_out = area(20640, RT, NSEQ)
        cs_out = area(20736, RT, NB, 3)
        cp_out = area(20976, RT, 3)
        mix_r = area(8640, KD, T)
        qp = area(0, 16, T)
        key = area(4608, 16, NKEY)
        acts = area(0, HALF, T)
        scor = [area(18432, 16, NKEY), area(20480, 16, NKEY), area(22528, 4, NKEY)]
        onek = area(ONEK_TILE * T, SLOTS, TOPK)
        cand = hid[:, :, 0:256]
        val = area(23040, 16, TOPK)
        idx = area(23296, 16, TOPK, dt=U32)
        idx_f = area(23552, 16, TOPK)
        best = area(23808, PH, TOPK)
        pos = area(23936, PH, TOPK, dt=U32)
        pa_f = area(24064, SLOTS)
        pb_f = area(24192, SLOTS)
        pa = area(24320, SLOTS, dt=U32)
        pb = area(24448, SLOTS, dt=U32)
        slot = area(24576, 3, SLOTS)
        ssum = area(24960, 2, PH)
        sel = area(24976, 3, T)
        minus_i2 = area(25840, T)
        oh_b = area(18432, 4, 4, NKEY)
        oh_a = area(20480, 4, 4, HALF)

        def pcol(name, a=0, b=None):
            lo, hi = PAR_COLS[name]
            return parm[:, lo + a:hi if b is None else lo + b]

        def ccol(name, parts=P):
            lo, hi = CON_COLS[name]
            return const[0:parts, lo:hi]

        ident, iota = ccol("ident"), ccol("iota")

        pu = ctx.enter_context(nc.psum_tensor("pu", [P, 4, 512], F32))
        pm = ctx.enter_context(nc.psum_tensor("pm", [P, 4, 512], F32))

        raw_full = [sem(f"raw_full{s}") for s in range(RING)]
        hi_done = sem("hi_done")
        lo_done = sem("lo_done")
        split_used = sem("split_used")
        raw_used = sem("raw_used")
        gate_used = sem("gate_used")
        pu_evac = sem("pu_evac")
        pv_evac = sem("pv_evac")
        vec = sem("vec")
        act_own = sem("act_own")
        (consts_in, ones_set, cond_ready, side_in, sq_ready, sum_ready, mean_ready, root_ready, hid_ready, hh_ready,
         hl_ready) = [sem(n) for n in (
            "consts_in", "ones_set", "cond_ready", "side_in", "sq_ready", "sum_ready", "mean_ready", "root_ready",
            "hid_ready", "hh_ready", "hl_ready")]
        (lr_ready, lrt_ready, z_ready, absz_ready, minz_ready, log_ready, cum_ready, exps_ready, dend_ready,
         edend_ready, ke_ready, qk_ready, tr_ready, tr_evac, sc_ready, sc_masked, o_ready, o_evac, ds_ready, s_new,
         kem_ready, st_used, stn_ready, osq_ready, osum_ready, omean_ready, oroot_ready, silu_ready,
         og_ready, gla_p_done) = [sem(n) for n in (
            "lr_ready", "lrt_ready", "z_ready", "absz_ready", "minz_ready", "log_ready", "cum_ready", "exps_ready",
            "dend_ready", "edend_ready", "ke_ready", "qk_ready", "tr_ready", "tr_evac", "sc_ready", "sc_masked",
            "o_ready", "o_evac", "ds_ready", "s_new", "kem_ready", "st_used", "stn_ready", "osq_ready",
            "osum_ready", "omean_ready", "oroot_ready", "silu_ready", "og_ready", "gla_p_done")]
        st_in = [sem(f"st_in{s}") for s in range(2)]
        st_out = [sem(f"st_out{s}") for s in range(2)]
        (rg_side, conv_ready, tanh_ready, sqrt_ready, sp_ready, gelu_y, lame_ready, hs_ready, hg_ready) = [
            sem(n) for n in ("rg_side", "conv_ready", "tanh_ready", "sqrt_ready", "sp_ready", "gelu_y",
                             "lame_ready", "hs_ready", "hg_ready")]
        (key_in, s_ready, s_evac, shift_ready, exp_ready, slot_ready, slot_t, sel_ready, oh_ready, oh_used,
         eq_ready, ob_act, ob_vec, abs_done, w_made, wh_ready, w_ready, lo_pool, ada_row_ready, ada_tr, mod_ready,
         out_ready, outs_done) = [sem(n) for n in (
            "key_in", "s_ready", "s_evac", "shift_ready", "exp_ready", "slot_ready", "slot_t", "sel_ready",
            "oh_ready", "oh_used", "eq_ready", "ob_act", "ob_vec", "abs_done", "w_made", "wh_ready",
            "w_ready", "lo_pool", "ada_row_ready", "ada_tr", "mod_ready", "out_ready", "outs_done")]
        MOVING = {"gla_in": 1, "gla_out": 2, "wq0": 3, "uv0": 3, "rg_in": 4, "rg_out": 5, "wq1": 6, "uv1": 6}

        srcs = {"ada_a": ada[0:16], "ada_b": ada[16:64], "ada_c": ada[64:96], "gla_in": gla_in, "gla_out": gla_out,
                "wq0": wq[0], "wq1": wq[1], "rg_in": rg_in, "gates": gates, "rg_out": rg_out}
        counts = {name: c for name, c, _ in SEGMENTS}
        order = [name for name, _, _ in SEGMENTS]
        LATE_WEIGHTS = [(), (0,), (1,), (2, 3)]
        GATE_OUTS = [3, 5]

        def freed(eng, name, c, first_half=False):
            if name == "gates":
                eng.wait_ge(gate_used, 5 * (c // 2) + GATE_OUTS[c % 2])
            elif name[:3] == "ada":
                eng.wait_ge(raw_used, c + (RAW[name] + 1))
            elif first_half:
                eng.wait_ge(lo_pool, c + (int(name[2]) * HALF + 1))
            else:
                eng.wait_ge(lo_done, c + (LOWS[name] + 1 - (HALF if name[:2] == "uv" else 0)))

        block = ctx.enter_context(nc.Block())

        @block.sync
        def _(sp_):
            for n, name in enumerate(order):
                total = counts[name]
                for s in range(RING):
                    if n:
                        freed(sp_, order[n - 1], counts[order[n - 1]] - RING + s)
                    src = u_tab[int(name[2]), s] if name[:2] == "uv" else srcs[name][s]
                    sp_.dma_start(raw[:, s, :], src).then_inc(raw_full[s], 16)
                if name == "gates":
                    for c in range(RING, total):
                        freed(sp_, name, c - RING)
                        sp_.dma_start(raw[:, c % RING, :], srcs[name][c]).then_inc(raw_full[c % RING], 16)
                elif name[:2] == "uv":
                    lay = int(name[2])
                    with sp_.Fori(1, HALF // RING) as i:
                        for s in range(RING):
                            freed(sp_, name, i * RING - RING + s, first_half=True)
                            sp_.dma_start(raw[:, s, :], u_tab[lay, i * RING + s]).then_inc(raw_full[s], 16)

                    def both(i, before_in_first):
                        for s in range(RING):
                            freed(sp_, name, i * RING + (HALF - RING + s), first_half=before_in_first)
                            src = u_tab[lay, i * 2 + (HALF + s // 2)] if s % 2 else v_tab[lay, i * 2 + s // 2]
                            sp_.dma_start(raw[:, s, :], src).then_inc(raw_full[s], 16)

                    both(0, True)
                    with sp_.Fori(1, HALF // 2) as i:
                        both(i, False)
                    with sp_.Fori(0, HALF // RING) as i:
                        for s in range(RING):
                            freed(sp_, name, i * RING + (3 * HALF - RING + s))
                            sp_.dma_start(raw[:, s, :], v_tab[lay, i * RING + (HALF + s)]).then_inc(raw_full[s], 16)
                elif total > RING:
                    with sp_.Fori(1, total // RING) as i:
                        for s in range(RING):
                            freed(sp_, name, i * RING - RING + s)
                            sp_.dma_start(raw[:, s, :], srcs[name][i * RING + s]).then_inc(raw_full[s], 16)

        @block.gpsimd
        def _(pool):
            def peer_pool(lay):
                m0 = SPLIT[f"uv{lay}"]
                with pool.Fori(0, HALF // RING) as i:
                    for s in range(RING):
                        pool.wait_ge(hi_done, i * RING + (m0 + s + 1))
                        pool.tensor_tensor(w_lo[:, s % 2, :], raw[:, s, :], w_hi[:, s % 2, :].bitcast(F32),
                                           ALU.subtract).then_inc(lo_pool, 1)
                for hf in range(2):
                    o0 = (lay * 2 + hf) * (T // 4)
                    with pool.Fori(0, T // 16) as i:
                        for r in range(4):
                            pool.wait_ge(eq_ready, i * 4 + (o0 + r + 1))
                            w4 = sel[:, 2, bass.ds(i * 16 + r * 4, 4)].unsqueeze(2).to_broadcast([P, 4, HALF])
                            pool.tensor_tensor(oh_a[:, r], oh_a[:, r], w4, ALU.mult).then_inc(oh_ready, 1)

            pool.memset(ones[:], 1.0).then_inc(ones_set, 1)
            pool.wait_ge(edend_ready, 1)
            pool.wait_ge(qk_ready, 1)
            pool.wait_ge(tr_evac, 15)
            for b in range(2):
                pool.dma_start(s_in[:, b, :], gla_state[b]).then_inc(st_in[b], 16)
            for b in range(NB):
                pool.wait_ge(stn_ready, HEADS * (b + 1))
                pool.dma_start(gla_s_out[b], s_in[:, b % 2, :]).then_inc(st_out[b % 2], 16)
                if b + 2 < NB:
                    pool.wait_ge(st_out[b % 2], 16 * (b // 2 + 1))
                    pool.dma_start(s_in[:, b % 2, :], gla_state[b + 2]).then_inc(st_in[b % 2], 16)
            pool.wait_ge(s_new, HEADS * NCH)
            pool.dma_start(gla_p_out, s_pr).then_inc(gla_p_done, 16)
            pool.wait_ge(og_ready, 1)
            pool.dma_start(key, keys[0]).then_inc(key_in, 16)
            peer_pool(0)
            pool.wait_ge(w_ready, NKEY)
            pool.dma_start(h0, h_state).then_inc(rg_side, 16)
            pool.dma_start(conv0, conv_state).then_inc(rg_side, 16)
            pool.dma_start(tail, rg_tail).then_inc(rg_side, 16)
            pool.wait_ge(hs_ready, 1)
            pool.dma_start(h_out, hl_out).then_inc(outs_done, 16)
            pool.dma_start(conv_s_out, cs_out).then_inc(outs_done, 16)
            pool.dma_start(conv_p_out, cp_out).then_inc(outs_done, 16)
            pool.dma_start(key, keys[1]).then_inc(key_in, 16)
            peer_pool(1)
            pool.wait_ge(out_ready, 1)
            pool.dma_start(y_out, hid[:]).then_inc(outs_done, 16)
            pool.wait_ge(outs_done, 16 * 4)
            pool.wait_ge(gla_p_done, 16)
            pool.wait_ge(st_out[0], 16 * NB // 2)
            pool.wait_ge(st_out[1], 16 * NB // 2)

        @block.scalar
        def _(act):
            own = [0]

            def link(ins):
                own[0] += 1
                ins.then_inc(act_own, 1)
                act.wait_ge(act_own, own[0])

            act.dma_start(cond[:], ct).then_inc(consts_in, 16)
            act.dma_start(parm[:], par).then_inc(consts_in, 16)
            act.dma_start(x[:], xt).then_inc(consts_in, 16)
            act.dma_start(const[:], con).then_inc(consts_in, 16)
            act.dma_start(lr_w, w_lr).then_inc(side_in, 16)
            act.dma_start(gate2, w_gate2).then_inc(side_in, 16)
            act.wait_ge(consts_in, 64)
            act.activation(cond[:], cond[:], ACT.Silu).then_inc(cond_ready, 1)

            def ada_out(first, last):
                for g in range(first, last):
                    act.wait_ge(raw_used, KD * (g + 1))
                    if g:
                        act.wait_ge(ada_tr, g)
                    act.activation(ada_row.rearrange("p (e n) -> p e n", e=2),
                                   pu[0:NSEQ, (g % 2) * 2:(g % 2) * 2 + 2, :], ACT.Copy).then_inc(ada_row_ready, 1)

            def high(s4, s2, full):
                act.wait_ge(raw_full[s4], full)
                act.activation(w_hi[:, s2, :], raw[:, s4, :], ACT.Copy).then_inc(hi_done, 1)

            def project(name, dest):
                total, m0, n0 = counts[name], SPLIT[name], STREAM[name]

                def group(i, first):
                    for s in range(4):
                        if not first or m0 + s >= 2:
                            act.wait_ge(split_used, i * 4 + (m0 + s - 1))
                        if not (first and s < 2):
                            act.activation(dest[:, i * 4 + (s - 2), :], pu[:, (s - 2) % 4, 0:T], ACT.Copy).then_inc(pu_evac, 1)
                        high(s, s % 2, i * 16 + (n0 // RING + 1) * 16)

                group(0, True)
                if total > 4:
                    with act.Fori(1, total // 4) as i:
                        group(i, False)
                for s in range(2):
                    act.wait_ge(split_used, m0 + total - 1 + s)
                    act.activation(dest[:, total - 2 + s, :], pu[:, 2 + s, 0:T], ACT.Copy).then_inc(pu_evac, 1)

            def norm_root(n):
                act.wait_ge(mean_ready, n + 1)
                act.activation(root[:], mean[:], ACT.Sqrt).then_inc(root_ready, 1)
                if n < 4:
                    act.wait_ge(hid_ready, n + 1)
                    act.activation(hid_hi[:], hid[:], ACT.Copy).then_inc(hh_ready, 1)

            def peer(lay):
                project(f"wq{lay}", qp)
                for n in range(9):
                    act.wait_ge(s_ready, lay * 9 + n + 1)
                    act.activation(scor[n // 4][:, 4 * (n % 4):4 * (n % 4) + 4, :],
                                   pm[:, n % 4, :].rearrange("p (a n) -> p a n", a=4), ACT.Copy).then_inc(s_evac, 1)

                name = f"uv{lay}"
                m0, n0, u0 = SPLIT[name], lay * NKEY, BANKED[name]
                full0 = (STREAM[name] // RING + 1) * 16

                def gelu(tile, s):
                    act.activation(acts[:, bass.ds(tile, 1), :], pu[:, s % 4, 0:T].unsqueeze(1),
                                   ACT.Gelu_apprx_tanh).then_inc(pu_evac, 1)

                def softmax_exp(tt):
                    act.wait_ge(shift_ready, lay * 3 + tt + 1)
                    n = SLOTS if tt < 2 else 32
                    act.activation(slot[:, 2, 0:n], slot[:, 2, 0:n], ACT.Exp).then_inc(exp_ready, 1)

                def u_only(i, first):
                    for s in range(4):
                        act.wait_ge(split_used, i * 4 + (m0 + s - 1))
                        high(s, s % 2, i * 16 + full0)
                        if not (first and s < 2):
                            gelu(i * 4 + (s - 2), s - 2)

                u_only(0, True)
                for first, last, tt in ((1, 5, 0), (5, 10, 1), (10, 14, 2)):
                    with act.Fori(first, last) as i:
                        u_only(i, False)
                    softmax_exp(tt)
                act.wait_ge(sel_ready, lay + 1)
                u_only(14, False)
                u_only(15, False)
                for s in range(2):
                    act.wait_ge(split_used, m0 + HALF - 1 + s)
                    gelu(HALF - 2 + s, 2 + s)

                def half_one_hots(hf):
                    o0 = (lay * 2 + hf) * (T // 4)

                    def sixteen(i, first):
                        for r in range(4):
                            if o0 or not first:
                                act.wait_ge(oh_used, i * 4 + (o0 + r - 3))
                            for t in range(2):
                                last = act.activation(oh_b[:, r, 2 + t, :], iota, ACT.Abs,
                                                      bias=minus_i2[:, bass.ds(i * 16 + (r * 4 + 2 + t), 1)])
                            last.then_inc(abs_done, 1)
                            act.wait_ge(abs_done, i * 4 + (o0 + r + 1))
                            act.activation(oh_b[:, r, 2:4, :], oh_b[:, r, 2:4, :], ACT.Relu, bias=1.0,
                                           scale=-1.0).then_inc(ob_act, 1)

                    act.wait_ge(sel_ready, lay + 1)
                    sixteen(0, True)
                    with act.Fori(1, T // 16) as i:
                        sixteen(i, False)

                def weight_high(tile, par, jj):
                    act.activation(wgt_hi[:, par, jj, :].unsqueeze(1), acts[:, bass.ds(tile, 1), :], ACT.Copy).then_inc(wh_ready, 1)

                def pairs(i, first=False, final=False):
                    for st in range(8):
                        m = i * 16 + (m0 + HALF + 2 * st)
                        full = i * 64 + (full0 + 256 + 16 * (st // 2))
                        act.wait_ge(split_used, m - 1)
                        high((2 * st) % 4, 0, full)
                        if not (final and st >= 4):
                            weight_high(i * 8 + (GRP + st), (st // 4 + 1) % 2, st % 4)
                        act.wait_ge(split_used, m)
                        high((2 * st + 1) % 4, 1, full)
                        if not (first and st == 0):
                            gelu(i * 8 + (st - 1), st - 1)

                def v_only(i, first=False, final=False):
                    for st in range(8):
                        m = i * 8 + (m0 + 3 * HALF + st)
                        act.wait_ge(split_used, m - 1)
                        high(st % 4, st % 2, i * 32 + (full0 + 768 + 16 * (st // 4)))
                        for jj in LATE_WEIGHTS[st % 4]:
                            if not (final and st >= 4):
                                weight_high(i * 8 + (st // 4 * GRP + GRP + jj), (st // 4 + 1) % 2, jj)

                half_one_hots(0)
                act.wait_ge(w_made, (lay * 2 + 1) * (T // 8))
                for j in range(GRP):
                    weight_high(j, 0, j)
                pairs(0, first=True)
                with act.Fori(1, 7) as i:
                    pairs(i)
                pairs(7, final=True)
                act.wait_ge(split_used, m0 + 3 * HALF)
                gelu(HALF - 1, 3)
                half_one_hots(1)
                act.wait_ge(w_made, (lay * 2 + 2) * (T // 8))
                for j in range(GRP):
                    weight_high(j, 0, j)
                v_only(0, first=True)
                with act.Fori(1, 7) as i:
                    v_only(i)
                v_only(7, final=True)

            ada_out(0, 2)
            norm_root(0)
            project("gla_in", proj)
            act.wait_ge(lr_ready, 1)
            act.activation(lr_t, pm[0:RANK, 0, 0:T], ACT.Copy).then_inc(lrt_ready, 1)
            act.wait_ge(z_ready, 1)
            for h in range(HEADS):
                last = act.activation(e_pos[:, h, :], pm[:, h, 0:T], ACT.Abs, bias=pcol("b_gate", h, h + 1))
            last.then_inc(absz_ready, 1)
            act.wait_ge(absz_ready, 1)
            link(act.activation(e_neg, e_pos, ACT.Exp, scale=-1.0))
            act.activation(e_neg, e_neg, ACT.Ln, bias=1.0).then_inc(log_ready, 1)
            act.wait_ge(cum_ready, 1)
            act.activation(e_pos, decay, ACT.Exp, scale=1.0 / TAU).then_inc(exps_ready, 1)
            act.activation(e_neg, decay, ACT.Exp, scale=-1.0 / TAU).then_inc(exps_ready, 1)
            act.wait_ge(dend_ready, 1)
            act.activation(k_end, k_end, ACT.Exp, scale=1.0 / TAU).then_inc(edend_ready, 1)
            ada_out(2, 8)
            for n in range(15):
                c, part = divmod(n, 3)
                rows = CH if c < NCH else 32
                act.wait_ge(tr_ready, n + 1)
                dst = v_tok[0:rows, c, part * 512:part * 512 + 512] if part < 2 else ke_tok[0:rows, c, :]
                act.activation(dst, pm[0:rows, n % 4, :], ACT.Copy).then_inc(tr_evac, 1)
            for c in range(NCH + 1):
                act.wait_ge(o_ready, c + 1)
                cols = slice(c * CH, (c + 1) * CH) if c < NCH else slice(SEQ, T)
                width = 8 * (CH if c < NCH else 32)
                act.activation(ot[:, :, cols], pm[:, 2 + c % 2, 0:width].rearrange("p (a t) -> p a t", a=8),
                               ACT.Copy).then_inc(o_evac, 1)
            act.activation(gt, gt, ACT.Silu).then_inc(silu_ready, 1)
            act.wait_ge(omean_ready, 1)
            act.activation(rms_t, rms_h, ACT.Sqrt).then_inc(oroot_ready, 1)
            act.wait_ge(og_ready, 1)
            act.activation(hid_hi[:], ot, ACT.Copy).then_inc(hh_ready, 1)
            project("gla_out", mix_g)
            norm_root(1)
            peer(0)

            norm_root(2)
            project("rg_in", area(0, 2 * RT, T))
            ada_out(8, 12)
            act.activation(sp[:, 1, :], pcol("lam"), ACT.Abs).then_inc(lame_ready, 1)
            act.wait_ge(lame_ready, 1)
            act.activation(sp[:, 1, :], sp[:, 1, :], ACT.Exp, scale=-1.0).then_inc(lame_ready, 1)
            for gate, (dst, bias) in enumerate(((g_r, "b_a"), (g_i, "b_x"))):
                for o in range(RT):
                    act.wait_ge(gate_used, gate * RT + o + 1)
                    act.activation(dst[:, o, :], pu[:, (gate * RT + o) % 4, 0:T], ACT.Sigmoid,
                                   bias=pcol(bias, o, o + 1)).then_inc(pu_evac, 1)
            act.wait_ge(sp_ready, 1)
            act.wait_ge(pu_evac, BANKED["gates"] + 2 * RT)
            for o in range(RT):
                last = act.activation(av[:, o, :], g_r[:, o, :], ACT.Tanh, scale=sp[:, 7, o:o + 1])
            last.then_inc(tanh_ready, 1)
            act.wait_ge(tanh_ready, 1)
            act.activation(mult, av, ACT.Sqrt).then_inc(sqrt_ready, 1)
            act.activation(yb, yb, ACT.Gelu_apprx_tanh).then_inc(gelu_y, 1)
            act.wait_ge(hg_ready, 1)
            act.activation(hid_hi[:], yb[:, 0:KD, :], ACT.Copy).then_inc(hh_ready, 1)
            project("rg_out", mix_r)
            norm_root(3)
            peer(1)
            norm_root(4)

        @block.tensor
        def _(pe):
            mm = pe.matmul

            def three(out, cols, kk, r_hi, r_lo, s2, n_k, stop=True):
                mm(out, w_hi[:, s2, cols], r_hi, start=(kk == 0), stop=False)
                mm(out, w_hi[:, s2, cols], r_lo, start=False, stop=False)
                return mm(out, w_lo[:, s2, cols], r_hi, start=False, stop=(stop and kk == n_k - 1))

            def chunk(out, s2):
                for kk in range(KD):
                    last = three(out, slice(kk * P, kk * P + P), kk, hid_hi[:, kk, :], hid_lo[:, kk, :], s2, KD)
                return last

            def squares(n):
                pe.wait_ge(sq_ready, n + 1)
                for kk in range(KD):
                    last = mm(pm[:, 0, 0:T], ones[:], hid[:, kk, :], start=(kk == 0), stop=(kk == KD - 1))
                last.then_inc(sum_ready, 1)

            def ada_sums(name, g0):
                full0, parts = (STREAM[name] // RING + 1) * 16, counts[name] // KD
                for g in range(g0, g0 + parts):
                    if g >= 2:
                        pe.wait_ge(mod_ready, g - 1)
                    for kk in range(KD):
                        pe.wait_ge(raw_full[kk % 4], full0 + ((g - g0) * 2 + kk // 4) * 16)
                        for e in range(2):
                            last = mm(pu[0:NSEQ, (g % 2) * 2 + e, :], cond[:, kk, :],
                                      raw[:, kk % 4, e * 512:e * 512 + 512], start=(kk == 0), stop=(kk == KD - 1))
                        last.then_inc(raw_used, 1)
                    if g > g0:
                        turn(g - 1)
                turn(g0 + parts - 1)

            def turn(g):
                pe.wait_ge(ada_row_ready, g + 1)
                for kk in range(KD):
                    last = pe.transpose(pu[:, (g % 2) * 2, kk * NSEQ:kk * NSEQ + NSEQ], ada_row[:, kk * P:kk * P + P],
                                        ident[0:NSEQ, 0:NSEQ])
                last.then_inc(ada_tr, 1)

            def project(name):
                l0, u0 = LOWS[name], BANKED[name]
                pe.wait_ge(hh_ready, MOVING[name])
                pe.wait_ge(hl_ready, MOVING[name])

                def group(i, first):
                    for s in range(4):
                        pe.wait_ge(lo_done, i * 4 + (l0 + s + 1))
                        if not first or u0 + s >= 4:
                            pe.wait_ge(pu_evac, i * 4 + (u0 + s - 3))
                        chunk(pu[:, s, 0:T], s % 2).then_inc(split_used, 1)

                group(0, True)
                with pe.Fori(1, counts[name] // 4) as i:
                    group(i, False)

            def peer(lay):
                squares(1 + 2 * lay)
                project(f"wq{lay}")
                pe.wait_ge(key_in, 16 * (lay + 1))
                pe.wait_ge(pu_evac, BANKED[f"wq{lay}"] + 16)
                for n in range(9):
                    if n >= 4:
                        pe.wait_ge(s_evac, lay * 9 + n - 3)
                    if n < 8:
                        for a in range(4):
                            hp = 4 * (n % 4) + a
                            last = mm(pm[:, n % 4, a * P:a * P + P], qp[:, hp, (n // 4) * P:(n // 4) * P + P], key[:, hp, :],
                                      start=True, stop=True)
                    else:
                        for hp in range(16):
                            at = hp // 4 * 32
                            last = mm(pm[at:at + 32, 0, (hp % 4) * P:(hp % 4) * P + P], qp[:, hp, SEQ:T], key[:, hp, :],
                                      start=True, stop=True)
                    last.then_inc(s_ready, 1)

                name = f"uv{lay}"
                m0, n0, u0, l0 = SPLIT[name], lay * NKEY, BANKED[name], LOWS[name]

                def turn_slots(tt):
                    pe.wait_ge(slot_ready, lay * 2 + tt + 1)
                    if tt == 0:
                        pe.wait_ge(s_evac, lay * 9 + 9)
                    for a in range(3):
                        last = pe.transpose(pm[:, tt, a * P:a * P + P], slot[:, a, :], ident)
                    last.then_inc(slot_t, 1)

                def u_first(i):
                    for s in range(4):
                        pe.wait_ge(hi_done, i * 4 + (m0 + s + 1))
                        pe.wait_ge(pu_evac, i * 4 + (u0 + s - 3))
                        for kk in range(KD):
                            mm(pu[:, s, 0:T], w_hi[:, s % 2, kk * P:kk * P + P], hid_hi[:, kk, :], start=(kk == 0), stop=False)
                            mm(pu[:, s, 0:T], w_hi[:, s % 2, kk * P:kk * P + P], hid_lo[:, kk, :], start=False, stop=False)
                        pe.wait_ge(lo_pool, i * 4 + (lay * HALF + s + 1))
                        for kk in range(KD):
                            last = mm(pu[:, s, 0:T], w_lo[:, s % 2, kk * P:kk * P + P], hid_hi[:, kk, :], start=False,
                                      stop=(kk == KD - 1))
                        last.then_inc(split_used, 1)

                for first, last, tt in ((0, 6, 0), (6, 12, 1), (12, 16, 2)):
                    with pe.Fori(first, last) as i:
                        u_first(i)
                    if tt < 2:
                        turn_slots(tt)

                def build_g(hf):
                    o0 = (lay * 2 + hf) * (T // 4)
                    e0 = (lay * 2 + hf) * (T // 8)

                    def sixteen(i, first):
                        for b in range(2):
                            if e0 or not first:
                                pe.wait_ge(w_made, i * 2 + (e0 + b - 1))
                            for h in range(2):
                                r = b * 2 + h
                                pe.wait_ge(ob_vec, i * 4 + (o0 + r + 1))
                                pe.wait_ge(ob_act, i * 4 + (o0 + r + 1))
                                pe.wait_ge(oh_ready, i * 4 + (o0 + r + 1))
                                for t in range(4):
                                    last = mm(pm[:, 2 + b, (h * 4 + t) * HALF:(h * 4 + t + 1) * HALF], oh_b[:, r, t, :],
                                              oh_a[:, r, t, :], start=True, stop=True)
                                last.then_inc(oh_used, 1)

                    sixteen(0, True)
                    with pe.Fori(1, T // 16) as i:
                        sixteen(i, False)

                def times_v(vo, l, s2, group, par, pair):
                    pe.wait_ge(lo_done, l + 1)
                    pe.wait_ge(w_ready, group * GRP + (n0 + GRP))
                    if not isinstance(vo, int) or vo >= 2:
                        pe.wait_ge(pv_evac, vo - 1)
                    for e in range(2):
                        bank = pair * 2 + e
                        for jj in range(GRP):
                            last = three(pm[:, bank, 0:T], slice((2 * jj + e) * P, (2 * jj + e) * P + P), jj,
                                         wgt_hi[:, par, jj, :], wgt_lo[:, par, jj, :], s2, GRP)
                    last.then_inc(split_used, 1)

                def pairs(i):
                    for st in range(8):
                        times_v(i * 8 + (n0 + st), i * 16 + (l0 + 2 * st), 0, i * 2 + st // 4, st // 4, st % 2)
                        pe.wait_ge(lo_done, i * 16 + (l0 + 2 * st + 2))
                        pe.wait_ge(pu_evac, i * 8 + (u0 + HALF + st - 3))
                        chunk(pu[:, st % 4, 0:T], 1).then_inc(split_used, 1)

                def v_only(i):
                    for st in range(8):
                        times_v(i * 8 + (n0 + HALF + st), i * 8 + (l0 + 2 * HALF + st), st % 2, i * 2 + (16 + st // 4), st // 4, st % 2)

                build_g(0)
                pairs(0)
                with pe.Fori(1, 8) as i:
                    pairs(i)
                pe.wait_ge(pv_evac, n0 + HALF)
                build_g(1)
                with pe.Fori(0, 8) as i:
                    v_only(i)

            pe.wait_ge(cond_ready, 1)
            ada_sums("ada_a", 0)
            pe.wait_ge(ones_set, 1)
            squares(0)
            pe.wait_ge(mod_ready, 2)
            project("gla_in")
            pe.wait_ge(side_in, 32)
            for kk in range(KD):
                last = mm(pm[0:RANK, 0, 0:T], lr_w[:, kk, :], hid[:, kk, :], start=(kk == 0), stop=(kk == KD - 1))
            last.then_inc(lr_ready, 1)
            pe.wait_ge(lrt_ready, 1)
            for h in range(HEADS):
                last = mm(pm[:, h, 0:T], gate2[:, h * P:h * P + P], lr_t, start=True, stop=True)
            last.then_inc(z_ready, 1)
            pe.wait_ge(pu_evac, BANKED["gla_in"] + 24)
            ada_sums("ada_b", 2)
            pe.wait_ge(mod_ready, 8)
            pe.wait_ge(minz_ready, 1)
            pe.wait_ge(absz_ready, 1)
            for n in range(15):
                c, part = divmod(n, 3)
                rows = CH if c < NCH else 32
                if part == 2 and c == 0:
                    pe.wait_ge(ke_ready, 1)
                if n >= 4:
                    pe.wait_ge(tr_evac, n - 3)
                for a in range(4):
                    src = vt[:, part * 4 + a, c * CH:c * CH + rows] if part < 2 else k_end[:, a, c * CH:c * CH + rows]
                    last = pe.transpose(pm[0:rows, n % 4, a * P:a * P + P], src, ident)
                last.then_inc(tr_ready, 1)
            pe.wait_ge(qk_ready, 1)
            pe.wait_ge(tr_evac, 15)
            for c in range(NCH):
                for h in range(HEADS):
                    last = mm(pm[0:CH, c // 2, ((c % 2) * 4 + h) * CH:((c % 2) * 4 + h + 1) * CH],
                              k[:, h, c * CH:(c + 1) * CH], q[:, h, c * CH:(c + 1) * CH], start=True, stop=True)
            for h in range(HEADS):
                last = mm(pu[0:32, 3, h * 32:h * 32 + 32], k[:, h, SEQ:T], q[:, h, SEQ:T], start=True, stop=True)
            last.then_inc(sc_ready, 1)
            pe.wait_ge(sc_masked, 2)
            for c in range(NCH):
                if c >= 2:
                    pe.wait_ge(o_evac, c - 1)
                for a in range(8):
                    last = mm(pm[:, 2 + c % 2, a * CH:(a + 1) * CH], v_tok[0:CH, c, a * P:a * P + P],
                              sc[:, c * 4 + a // 2, :], start=(a == 0), stop=(c == 0 and a == 7), skip_group_check=True)
                if c:
                    pe.wait_ge(s_new, HEADS * c)
                    for a in range(8):
                        last = mm(pm[:, 2 + c % 2, a * CH:(a + 1) * CH], s_pr[:, a // 2, (a % 2) * P:(a % 2) * P + P],
                                  q[:, a // 2, c * CH:(c + 1) * CH], start=False, stop=(a == 7), skip_group_check=True)
                last.then_inc(o_ready, 1)
                for h in range(HEADS):
                    last = mm(pu[:, h // 2, (h % 2) * HDV:(h % 2 + 1) * HDV], ke_tok[0:CH, c, h * P:h * P + P],
                              v_tok[0:CH, c, h * HDV:(h + 1) * HDV], start=True, stop=True)
                last.then_inc(ds_ready, 1)
            for a in range(8):
                if a == 0:
                    pe.wait_ge(o_evac, 3)
                mm(pm[:, 2, a * 32:a * 32 + 32], v_tok[0:32, NCH, a * P:a * P + P], sc_s[:, a // 2, :],
                   start=(a == 0), stop=False, skip_group_check=True)
            pe.wait_ge(s_new, HEADS * NCH)
            for b in range(NB):
                pe.wait_ge(st_in[b % 2], 16 * (b // 2 + 1))
                for a in range(8):
                    last = mm(pm[:, 2, a * 32 + b * NT:a * 32 + b * NT + NT],
                              s_in[:, b % 2, a * P:a * P + P], q[:, a // 2, SEQ + b * NT:SEQ + b * NT + NT],
                              start=False, stop=(b == NB - 1 and a == 7), skip_group_check=True)
                if b == NB - 1:
                    last.then_inc(o_ready, 1)
                pe.wait_ge(kem_ready, b + 1)
                if b >= 2:
                    pe.wait_ge(stn_ready, HEADS * (b - 1))
                for h in range(HEADS):
                    last = mm(pu[:, (b % 2) * 2 + h // 2, (h % 2) * HDV:(h % 2 + 1) * HDV],
                              ke_m[:, b % 2, h * P:h * P + P], v_tok[0:32, NCH, h * HDV:(h + 1) * HDV],
                              start=True, stop=True)
                last.then_inc(st_used, 1)
            pe.wait_ge(osq_ready, 1)
            for h in range(HEADS):
                for e in range(2):
                    last = mm(pm[:, h, 0:T], ones[:], hid[:, 2 * h + e, :], start=(e == 0), stop=(e == 1))
            last.then_inc(osum_ready, 1)
            project("gla_out")
            peer(0)

            squares(2)
            project("rg_in")
            pe.wait_ge(pu_evac, BANKED["gates"])
            ada_sums("ada_c", 8)
            pe.wait_ge(mod_ready, 12)
            pe.wait_ge(conv_ready, 1)
            for c in range(8):
                gate, sg, part = c // 4, c // 2 % 2, c % 2
                pe.wait_ge(raw_full[c % 4], (STREAM["gates"] // RING + 1 + c // 4) * 16)
                pairs = GATE_PAIRS[part]
                for n, (src, dst) in enumerate(pairs):
                    o = gate * RT + sg * 5 + dst
                    first = n == 0 or pairs[n - 1][1] != dst
                    done = n == len(pairs) - 1 or pairs[n + 1][1] != dst
                    if first:
                        pe.wait_ge(pu_evac, BANKED["gates"] + o - 3)
                    last = mm(pu[:, o % 4, 0:T], raw[:, c % 4, n * P:n * P + P], xc[:, sg * 5 + src, :],
                              start=first, stop=done)
                    if done:
                        last.then_inc(gate_used, 1)
            pe.wait_ge(hh_ready, MOVING["rg_out"])
            pe.wait_ge(hl_ready, MOVING["rg_out"])
            pe.wait_ge(rg_side, 48)
            for o in range(KD):
                pe.wait_ge(lo_done, LOWS["rg_out"] + o + 1)
                pe.wait_ge(pu_evac, BANKED["rg_out"] + o - 3)
                for e in range(2):
                    mm(pu[:, o % 4, 0:T], tail[:, e, o * P:o * P + P], yb[:, KD + e, :], start=(e == 0), stop=False)
                for kk in range(KD):
                    last = three(pu[:, o % 4, 0:T], slice(kk * P, kk * P + P), kk + 1, hid_hi[:, kk, :],
                                 hid_lo[:, kk, :], o % 2, KD + 1)
                last.then_inc(split_used, 1)
            peer(1)
            squares(4)

        @block.vector
        def _(dve):
            own = [0]
            tt_, ts, stt = dve.tensor_tensor, dve.tensor_scalar, dve.scalar_tensor_tensor

            def link(ins):
                own[0] += 1
                ins.then_inc(vec, 1)
                dve.wait_ge(vec, own[0])

            def bc(v, *shape):
                for axis in range(len(v.shape), len(shape)):
                    v = v.unsqueeze(axis)
                return v.to_broadcast(list(shape))

            def samples(v):
                return v[:, :, SEQ:T].rearrange("p k (b t) -> p k b t", b=NB)

            def low(m, s4, s2):
                dve.wait_ge(hi_done, m + 1)
                tt_(w_lo[:, s2, :], raw[:, s4, :], w_hi[:, s2, :].bitcast(F32), ALU.subtract).then_inc(lo_done, 1)

            def lows(name):
                with dve.Fori(0, counts[name] // 4) as i:
                    for s in range(4):
                        low(i * 4 + (SPLIT[name] + s), s, s % 2)

            def moving_low(src, n):
                dve.wait_ge(hh_ready, n)
                tt_(hid_lo[:], src, hid_hi[:].bitcast(F32), ALU.subtract).then_inc(hl_ready, 1)

            def norm(n, gain, lay=0, j_shift=0):
                tt_(hid[:], x[:], x[:], ALU.mult).then_inc(sq_ready, 1)
                if n < 4:
                    link(stt(coef[:], mod[:, lay, j_shift + 1], 1.0, bc(gain, P, KD, NSEQ), ALU.add, ALU.mult))
                dve.wait_ge(sum_ready, n + 1)
                ts(mean[:], pm[:, 0, 0:T], 1.0 / D, EPS, ALU.mult, ALU.add).then_inc(mean_ready, 1)
                dve.wait_ge(mean_ready, n + 1)
                dve.wait_ge(root_ready, n + 1)
                inverse_root(root[:], mean[:], newt[:])
                link(tt_(hid[:], x[:], root[:].unsqueeze(1).to_broadcast([P, KD, T]), ALU.mult))
                if n == 4:
                    tt_(hid[:], hid[:], bc(gain, P, KD, T), ALU.mult).then_inc(out_ready, 1)
                    return
                for kk in range(KD):
                    last = ts(hid[:, kk, 0:SEQ], hid[:, kk, 0:SEQ], coef[:, kk, 0:1], mod[:, lay, j_shift, kk, 0:1],
                              ALU.mult, ALU.add)
                link(tt_(samples(hid[:]), samples(hid[:]), bc(coef[:, :, 1:NSEQ], P, KD, NB, NT), ALU.mult))
                tt_(samples(hid[:]), samples(hid[:]), bc(mod[:, lay, j_shift, :, 1:NSEQ], P, KD, NB, NT),
                    ALU.add).then_inc(hid_ready, 1)
                dve.wait_ge(hid_ready, n + 1)
                moving_low(hid[:], {0: 1, 1: 3, 2: 4, 3: 6}[n])

            def inverse_root(r, m, t):
                link(dve.reciprocal(r, r))
                link(tt_(t, r, r, ALU.mult))
                link(tt_(t, t, m, ALU.mult))
                link(ts(t, t, -0.5, 1.5, ALU.mult, ALU.add))
                link(tt_(r, r, t, ALU.mult))

            def residual(src, lay, j_gate):
                for kk in range(KD):
                    stt(x[:, kk, 0:SEQ], src[:, kk, 0:SEQ], mod[:, lay, j_gate, kk, 0:1], x[:, kk, 0:SEQ],
                        ALU.mult, ALU.add)
                link(tt_(samples(src), samples(src), bc(mod[:, lay, j_gate, :, 1:NSEQ], P, KD, NB, NT), ALU.mult))
                link(tt_(samples(x[:]), samples(x[:]), samples(src), ALU.add))

            def top16(values, n, width, out, out_i):
                for part in range(2):
                    at = slice(part * 8, part * 8 + 8)
                    for a in range(n):
                        last = dve.max(out[:, a, at], values[:, a, 0:width])
                    link(last)
                    for a in range(n):
                        last = dve.max_index(out_i[:, a, at], out[:, a, at], values[:, a, 0:width])
                    if part == 0:
                        for a in range(n):
                            last = dve.match_replace(values[:, a, 0:width], out[:, a, at], values[:, a, 0:width], LOWEST)
                    link(last)

            def mods(first, last):
                for g in range(first, last):
                    dve.wait_ge(ada_tr, g + 1)
                    tt_(mod[:, g // 6, g % 6], pu[:, (g % 2) * 2, 0:KD * NSEQ].rearrange("p (k b) -> p k b", k=KD),
                        bc(pcol("ada_b", g * KD, g * KD + KD), P, KD, NSEQ), ALU.add).then_inc(mod_ready, 1)

            def route(lay, tt):
                heads_n = PH if tt < 2 else 2
                slots_n = heads_n * TOPK
                dve.wait_ge(s_evac, lay * 9 + (4, 8, 9)[tt])
                top16(scor[tt], 2 * heads_n, NKEY, val, idx)
                dve.tensor_copy(idx_f[:, 0:2 * heads_n], idx[:, 0:2 * heads_n])
                pair = val.rearrange("p (h two) a -> p h two a", two=2)
                for h in range(heads_n):
                    last = tt_(cand[:, h, :].rearrange("p (a b) -> p a b", a=TOPK), bc(pair[:, h, 0, :], P, TOPK, TOPK),
                               pair[:, h, 1, :].unsqueeze(1).to_broadcast([P, TOPK, TOPK]), ALU.add)
                link(last)
                top16(cand, heads_n, 256, best, pos)
                if tt:
                    dve.wait_ge(slot_t, lay * 2 + tt)
                by_head = slot[:, 2, 0:slots_n].rearrange("p (h a) -> p h a", h=heads_n)
                tt_(by_head, best[:, 0:heads_n], best[:, 0:heads_n, 0:1].to_broadcast([P, heads_n, TOPK]),
                    ALU.subtract).then_inc(shift_ready, 1)
                flat = pos[:, 0:heads_n].rearrange("p h a -> p (h a)")
                ts(pa[:, 0:slots_n], flat, 4, None, ALU.logical_shift_right)
                link(ts(pb[:, 0:slots_n], flat, 15, None, ALU.bitwise_and))
                dve.tensor_copy(pa_f[:, 0:slots_n], pa[:, 0:slots_n])
                link(dve.tensor_copy(pb_f[:, 0:slots_n], pb[:, 0:slots_n]))
                place = iota[:, 0:TOPK].unsqueeze(1).to_broadcast([P, slots_n, TOPK])
                pair_i = idx_f.rearrange("p (h two) a -> p h two a", two=2)
                for which, src in enumerate((pa_f, pb_f)):
                    link(tt_(onek[:, 0:slots_n], bc(src[:, 0:slots_n], P, slots_n, TOPK), place, ALU.is_equal))
                    for h in range(heads_n):
                        rng = onek[:, h * TOPK:(h + 1) * TOPK, :]
                        last = tt_(rng, rng, pair_i[:, h, which, :].unsqueeze(1).to_broadcast([P, TOPK, TOPK]), ALU.mult)
                    link(last)
                    link(dve.tensor_reduce(slot[:, which, 0:slots_n], onek[:, 0:slots_n], AX_X, ALU.add))
                dve.wait_ge(exp_ready, lay * 3 + tt + 1)
                link(dve.tensor_reduce(ssum[:, 0, 0:heads_n], by_head, AX_X, ALU.add))
                link(dve.reciprocal(ssum[:, 1, 0:heads_n], ssum[:, 0, 0:heads_n]))
                last = tt_(by_head, by_head, bc(ssum[:, 1, 0:heads_n], P, heads_n, TOPK), ALU.mult)
                if tt < 2:
                    last.then_inc(slot_ready, 1)
                else:
                    link(last)

            def peer(lay):
                norm(1 + 2 * lay, pcol("ffn_g", lay * KD, lay * KD + KD), lay, 3)
                lows(f"wq{lay}")
                for tt in range(3):
                    route(lay, tt)
                for a in range(3):
                    dve.transpose(sel[:, a, SEQ:T], slot[:, a, 0:NB * NT])
                for tt in range(2):
                    dve.wait_ge(slot_t, lay * 2 + tt + 1)
                    last = dve.tensor_copy(sel[:, :, tt * P:tt * P + P], pm[:, tt, 0:384].rearrange("p (a t) -> p a t", a=3))
                link(last)
                ts(minus_i2, sel[:, 1, :], -1.0, None, ALU.mult).then_inc(sel_ready, 1)
                link(dve.memset(hid[:], 0.0))
                name = f"uv{lay}"
                m0, n0, u0 = SPLIT[name], lay * NKEY, BANKED[name]

                def weigh_by_g(hf):
                    o0, e0 = (lay * 2 + hf) * (T // 4), (lay * 2 + hf) * (T // 8)
                    firsts = iota[:, hf * HALF:(hf + 1) * HALF].unsqueeze(1).to_broadcast([P, 4, HALF])
                    seconds = iota.unsqueeze(1).to_broadcast([P, 2, NKEY])

                    def rows(i, r, first):
                        if o0 or not first:
                            dve.wait_ge(oh_used, i * 4 + (o0 + r - 3))
                        tt_(oh_a[:, r], firsts, sel[:, 0, bass.ds(i * 16 + 4 * r, 4)].unsqueeze(2).to_broadcast([P, 4, HALF]),
                            ALU.is_equal).then_inc(eq_ready, 1)
                        tt_(oh_b[:, r, 0:2, :], seconds,
                            sel[:, 1, bass.ds(i * 16 + 4 * r, 2)].unsqueeze(2).to_broadcast([P, 2, NKEY]),
                            ALU.is_equal).then_inc(ob_vec, 1)

                    def times_g(i, b):
                        dve.wait_ge(oh_used, i * 4 + (o0 + 2 * b + 2))
                        eight = acts[:, :, bass.ds(i * 16 + 8 * b, 8)]
                        tt_(eight, eight, pm[:, 2 + b, :].rearrange("p (t i) -> p i t", t=8), ALU.mult).then_inc(w_made, 1)

                    def sixteen(i, first):
                        rows(i, 0, first)
                        rows(i, 1, first)
                        if first:
                            dve.wait_ge(pu_evac, u0 + (hf + 1) * HALF)
                        else:
                            times_g(i - 1, 0)
                        rows(i, 2, first)
                        rows(i, 3, first)
                        if not first:
                            times_g(i - 1, 1)

                    sixteen(0, True)
                    with dve.Fori(1, T // 16) as i:
                        sixteen(i, False)
                    times_g(T // 16 - 1, 0)
                    times_g(T // 16 - 1, 1)

                def weight_low(tile, n, par, jj):
                    dve.wait_ge(wh_ready, n + 1)
                    tt_(wgt_lo[:, par, jj, :].unsqueeze(1), acts[:, bass.ds(tile, 1), :],
                        wgt_hi[:, par, jj, :].bitcast(F32).unsqueeze(1), ALU.subtract).then_inc(w_ready, 1)

                def add_v(done, st):
                    dve.wait_ge(split_used, done)
                    two, banks = (st % 4) * 2, (st % 2) * 2
                    tt_(hid[:, two:two + 2, :], hid[:, two:two + 2, :], pm[:, banks:banks + 2, 0:T],
                        ALU.add).then_inc(pv_evac, 1)

                def pairs(i, first=False, final=False):
                    for st in range(8):
                        m = i * 16 + (m0 + HALF + 2 * st)
                        if not (first and st == 0):
                            add_v(m - 1, st - 1)
                        low(m, (2 * st) % 4, 0)
                        if not (final and st >= 4):
                            weight_low(i * 8 + (GRP + st), i * 8 + (n0 + GRP + st), (st // 4 + 1) % 2, st % 4)
                        low(m + 1, (2 * st + 1) % 4, 1)

                def v_only(i, first=False, final=False):
                    for st in range(8):
                        m = i * 8 + (m0 + 3 * HALF + st)
                        if not (first and st < 2):
                            add_v(m - 1, st - 2)
                        low(m, st % 4, st % 2)
                        for jj in LATE_WEIGHTS[st % 4]:
                            at = st // 4 * GRP + GRP + jj
                            if not (final and st >= 4):
                                weight_low(i * 8 + at, i * 8 + (n0 + HALF + at), (st // 4 + 1) % 2, jj)

                weigh_by_g(0)
                for j in range(GRP):
                    weight_low(j, n0 + j, 0, j)
                pairs(0, first=True)
                with dve.Fori(1, 7) as i:
                    pairs(i)
                pairs(7, final=True)
                add_v(m0 + 3 * HALF - 1, 7)
                weigh_by_g(1)
                for j in range(GRP):
                    weight_low(j, n0 + HALF + j, 0, j)
                v_only(0, first=True)
                with dve.Fori(1, 7) as i:
                    v_only(i)
                v_only(7, final=True)
                for late in (1, 0):
                    add_v(m0 + 4 * HALF - late, 7 - late)
                dve.wait_ge(pv_evac, n0 + NKEY)
                residual(hid[:], lay, 5)

            dve.wait_ge(consts_in, 64)
            mods(0, 2)
            dve.wait_ge(mod_ready, 2)
            norm(0, pcol("mix_g", 0, KD), 0, 0)
            lows("gla_in")
            dve.wait_ge(absz_ready, 1)
            for h in range(HEADS):
                last = ts(decay[:, h, :], pm[:, h, 0:T], pcol("b_gate", h, h + 1), 0.0, ALU.add, ALU.min)
            last.then_inc(minz_ready, 1)
            dve.wait_ge(minz_ready, 1)
            dve.wait_ge(log_ready, 1)
            link(tt_(decay, decay, e_neg, ALU.subtract))
            for h in range(HEADS):
                last = dve.tensor_tensor_scan(decay[:, h, :], ccol("keep"), decay[:, h, :], 0.0, ALU.mult, ALU.add)
            last.then_inc(cum_ready, 1)
            dve.wait_ge(cum_ready, 1)
            for h in range(HEADS):
                b4 = decay[:, h, 0:SEQ].rearrange("p (c t) -> p c t", c=NCH)
                tt_(k_end[:, h, 0:SEQ].rearrange("p (c t) -> p c t", c=NCH),
                    b4[:, :, CH - 1:CH].to_broadcast([P, NCH, CH]), b4, ALU.subtract)
                s4 = decay[:, h, SEQ:T].rearrange("p (b t) -> p b t", b=NB)
                last = tt_(k_end[:, h, SEQ:T].rearrange("p (b t) -> p b t", b=NB),
                           s4[:, :, NT - 1:NT].to_broadcast([P, NB, NT]), s4, ALU.subtract)
            last.then_inc(dend_ready, 1)
            dve.wait_ge(edend_ready, 1)
            dve.wait_ge(pu_evac, BANKED["gla_in"] + 24)
            tt_(k_end, k_end, k, ALU.mult).then_inc(ke_ready, 1)
            dve.wait_ge(exps_ready, 2)
            stt(q, q, float(P) ** -0.5, e_pos, ALU.mult, ALU.mult)
            tt_(k, k, e_neg, ALU.mult).then_inc(qk_ready, 1)
            mods(2, 8)
            dve.wait_ge(mod_ready, 8)
            dve.wait_ge(sc_ready, 1)
            for c2 in range(2):
                tt_(sc[:, c2 * 8:c2 * 8 + 8, :], pm[0:CH, c2, :].rearrange("p (a t) -> p a t", a=8),
                    ccol("causal", CH).unsqueeze(1).to_broadcast([CH, 8, CH]), ALU.mult).then_inc(sc_masked, 1)
            tt_(sc_s, pu[0:32, 3, 0:P].rearrange("p (a t) -> p a t", a=HEADS),
                ccol("sample_causal", 32).unsqueeze(1).to_broadcast([32, HEADS, 32]), ALU.mult).then_inc(sc_masked, 1)
            for c in range(NCH):
                dve.wait_ge(ds_ready, c + 1)
                if c:
                    dve.wait_ge(o_ready, c + 1)
                    dve.wait_ge(s_new, HEADS * c)
                for h in range(HEADS):
                    add = pu[:, h // 2, (h % 2) * HDV:(h % 2 + 1) * HDV]
                    end = c * CH + CH - 1
                    if c == 0:
                        dve.tensor_copy(s_pr[:, h, :], add).then_inc(s_new, 1)
                    else:
                        stt(s_pr[:, h, :], s_pr[:, h, :], e_pos[:, h, end:end + 1], add, ALU.mult, ALU.add).then_inc(s_new, 1)
            for b in range(NB):
                if b >= 2:
                    dve.wait_ge(st_used, b - 1)
                ts(ke_m[:, b % 2, :], ke_tok[0:32, NCH, :], ccol("seq_mask", 32)[:, b:b + 1], None,
                   ALU.mult).then_inc(kem_ready, 1)
                dve.wait_ge(st_used, b + 1)
                for h in range(HEADS):
                    s_v = s_in[:, b % 2, h * HDV:(h + 1) * HDV]
                    end = SEQ + b * NT + NT - 1
                    stt(s_v, s_v, e_pos[:, h, end:end + 1],
                        pu[:, (b % 2) * 2 + h // 2, (h % 2) * HDV:(h % 2 + 1) * HDV], ALU.mult,
                        ALU.add).then_inc(stn_ready, 1)
            dve.wait_ge(o_evac, NCH + 1)
            tt_(hid[:], ot, ot, ALU.mult).then_inc(osq_ready, 1)
            dve.wait_ge(osum_ready, 1)
            ts(rms_h, pm[:, :, 0:T], 1.0 / HDV, EPS, ALU.mult, ALU.add).then_inc(omean_ready, 1)
            dve.wait_ge(omean_ready, 1)
            dve.wait_ge(oroot_ready, 1)
            inverse_root(rms_t, rms_h, decay)
            heads = ot.rearrange("p (h e) t -> p h e t", e=2)
            for e in range(2):
                last = stt(heads[:, :, e, :], heads[:, :, e, :], pcol("onorm_g", e, e + 1), rms_t, ALU.mult, ALU.mult)
            link(last)
            dve.wait_ge(silu_ready, 1)
            tt_(ot, ot, gt, ALU.mult).then_inc(og_ready, 1)
            dve.wait_ge(og_ready, 1)
            moving_low(ot, 2)
            lows("gla_out")
            dve.wait_ge(pu_evac, BANKED["gla_out"] + 8)
            residual(mix_g, 0, 2)
            peer(0)

            norm(2, pcol("mix_g", KD, 2 * KD), 1, 0)
            lows("rg_in")
            dve.wait_ge(pu_evac, BANKED["rg_in"] + 20)
            dve.wait_ge(rg_side, 48)
            cw = pcol("conv_w")
            for o in range(RT):
                last = ts(xc[:, o, :], xb[:, o, :], cw[:, 3 * RT + o:3 * RT + o + 1], pcol("conv_b", o, o + 1),
                          ALU.mult, ALU.add)
            dve.tensor_copy(xs[:, :, :, 0:3], conv0)
            link(dve.tensor_copy(xs[:, :, :, 3:7], samples(xb)))
            for tap in range(3):
                back = 3 - tap
                for o in range(RT):
                    last = stt(xc[:, o, back:SEQ], xb[:, o, 0:SEQ - back], cw[:, tap * RT + o:tap * RT + o + 1],
                               xc[:, o, back:SEQ], ALU.mult, ALU.add)
                link(tt_(tmp_s, xs[:, :, :, tap:tap + 4], bc(cw[:, tap * RT:(tap + 1) * RT], P, RT, NB, NT), ALU.mult))
                link(tt_(samples(xc), samples(xc), tmp_s, ALU.add))
                mods(8 + tap, 9 + tap)
            mods(11, 12)
            dve.wait_ge(mod_ready, 12)
            dve.tensor_copy(cs_out, xs[:, :, :, 4:7])
            dve.tensor_copy(cp_out, xb[:, :, SEQ - 3:SEQ]).then_inc(conv_ready, 1)
            dve.wait_ge(lame_ready, 2)
            link(ts(sp[:, 2, :], sp[:, 1, :], 2.0, None, ALU.add))
            link(dve.reciprocal(sp[:, 2, :], sp[:, 2, :]))
            link(tt_(sp[:, 3, :], sp[:, 1, :], sp[:, 2, :], ALU.mult))
            link(tt_(sp[:, 4, :], sp[:, 3, :], sp[:, 3, :], ALU.mult))
            link(ts(sp[:, 5, :], sp[:, 4, :], 1.0 / 17, 1.0 / 15, ALU.mult, ALU.add))
            for odd in (13, 11, 9, 7, 5, 3, 1):
                link(tt_(sp[:, 5, :], sp[:, 5, :], sp[:, 4, :], ALU.mult))
                link(ts(sp[:, 5, :], sp[:, 5, :], 1.0 / odd, None, ALU.add))
            link(tt_(sp[:, 5, :], sp[:, 5, :], sp[:, 3, :], ALU.mult))
            link(ts(sp[:, 6, :], pcol("lam"), -4.0, 0.0, ALU.mult, ALU.max))
            stt(sp[:, 7, :], sp[:, 5, :], 8.0, sp[:, 6, :], ALU.mult, ALU.add).then_inc(sp_ready, 1)
            dve.wait_ge(tanh_ready, 1)
            link(ts(g_r, av, -1.0, -1.0, ALU.mult, ALU.add))
            link(dve.reciprocal(g_r, g_r))
            dve.wait_ge(sqrt_ready, 1)
            stt(av, av, 1.0, g_r, ALU.subtract, ALU.mult)
            link(stt(mult, mult, -2.0, g_r, ALU.mult, ALU.mult))
            dve.memset(av[:, :, 0:1], 0.0)
            link(dve.memset(mult[:, :, 0:1], 1.0))
            link(tt_(mult, mult, g_i, ALU.mult))
            link(tt_(mult, mult, xc, ALU.mult))
            a0, b0 = samples(av)[:, :, :, 0], samples(mult)[:, :, :, 0]
            link(tt_(h0, a0, h0, ALU.mult))
            link(tt_(b0, b0, h0, ALU.add))
            link(dve.memset(a0, 0.0))
            link(dve.tensor_tensor_scan(g_r.rearrange("p a t -> p (a t)"), av.rearrange("p a t -> p (a t)"),
                                        mult.rearrange("p a t -> p (a t)"), 0.0, ALU.mult, ALU.add))
            dve.tensor_copy(hl_out[:, :, 0:1], g_r[:, :, SEQ - 1:SEQ])
            dve.tensor_copy(hl_out[:, :, 1:NSEQ], samples(g_r)[:, :, :, NT - 1]).then_inc(hs_ready, 1)
            dve.wait_ge(gelu_y, 1)
            tt_(yb, yb, g_r, ALU.mult).then_inc(hg_ready, 1)
            dve.wait_ge(hg_ready, 1)
            moving_low(yb[:, 0:KD, :], 5)
            lows("rg_out")
            dve.wait_ge(pu_evac, BANKED["rg_out"] + 8)
            residual(mix_r, 1, 2)
            peer(1)
            norm(4, pcol("final_g"))


_PARAMS = ["xt", "ct", "par", "con", "ada", "gla_in", "w_lr", "w_gate2", "gla_out", "wq", "keys", "u_tab", "v_tab",
           "rg_in", "gates", "rg_out", "rg_tail", "gla_state", "h_state", "conv_state"]
_OUTS = [("y", (P, KD, T)), ("gla_p", (P, HEADS, HDV)), ("gla_s", (NB, P, D)), ("h", (P, RT, NSEQ)),
         ("conv_p", (P, RT, 3)), ("conv_s", (P, RT, NB, 3))]


def kernel(**inputs):
    import numpy as np
    import concourse.bacc as bacc
    from concourse.bass_utils import run_bass_kernel_spmd

    w = {n: np.asarray(a) for n, a in inputs.items()}

    def chunks(a):
        kk, n = a.shape[0] // P, a.shape[1] // P
        return a.reshape(kk, P, n, P).transpose(2, 1, 0, 3).reshape(n, P, kk * P)

    def cols(a):
        return a.reshape(-1, P).T

    tokens = np.concatenate([w["x_prompt"].reshape(SEQ, D), w["x_sample"].reshape(NB * NT, D)])
    cond = np.concatenate([w["c_prompt"], w["c_sample"]])
    parts = {"ada_b": w["ada_b"], "mix_g": w["norm_mix_g"], "ffn_g": w["norm_ffn_g"], "final_g": w["final_norm_g"],
             "b_gate": w["gla_b_gate"], "onorm_g": w["gla_onorm_g"], "lam": w["rg_lambda"], "b_a": w["rg_b_a"],
             "b_x": w["rg_b_x"], "conv_w": w["rg_conv_w"], "conv_b": w["rg_conv_b"]}
    seq_of = np.arange(NB * NT) // NT
    keep = np.ones(T, np.float32)
    keep[0:SEQ:CH] = 0
    keep[SEQ::NT] = 0
    con = np.zeros((P, CON_N), np.float32)
    for name, v in (("ident", np.eye(P)), ("iota", np.tile(np.arange(P), (P, 1))), ("keep", np.tile(keep, (P, 1))),
                    ("causal", np.triu(np.ones((CH, CH)))),
                    ("sample_causal", np.triu(np.ones((32, 32))) * (seq_of[:, None] == seq_of[None])),
                    ("seq_mask", seq_of[:, None] == np.arange(NB)[None])):
        con[:v.shape[0], CON_COLS[name][0]:CON_COLS[name][1]] = v
    gates = np.zeros((8, P, 8, P), np.float32)
    for n, name in enumerate(("rg_w_a", "rg_w_x")):
        for sg in range(2):
            dense = np.zeros((640, 640), np.float32)
            for b in range(4):
                dense[b * 160:(b + 1) * 160, b * 160:(b + 1) * 160] = w[name][0, sg * 4 + b]
            for part in range(2):
                for at, (src, dst) in enumerate(GATE_PAIRS[part]):
                    gates[n * 4 + sg * 2 + part, :, at] = dense[src * P:(src + 1) * P, dst * P:(dst + 1) * P]
    main_in = w["gla_w_in"][0][:, :3 * D]
    arrays = {
        "xt": tokens.reshape(T, KD, P).transpose(2, 1, 0),
        "ct": cond.reshape(NSEQ, KD, P).transpose(2, 1, 0),
        "par": np.concatenate([cols(parts[n]) for n in PAR_COLS], axis=1),
        "con": con,
        "ada": w["ada_w"].reshape(2, KD, P, 6, D).transpose(0, 3, 1, 2, 4).reshape(96, P, D),
        "gla_in": chunks(main_in),
        "w_lr": w["gla_w_in"][0][:, 3 * D:].reshape(KD, P, RANK).transpose(1, 0, 2),
        "w_gate2": w["gla_w_gate2"][0],
        "gla_out": chunks(w["gla_w_out"][0]),
        "wq": np.stack([chunks(w["peer_w_q"][i]) for i in range(2)]),
        "keys": w["peer_sub_keys"].reshape(2, 16, NKEY, P).transpose(0, 3, 1, 2),
        "u_tab": w["peer_u"].reshape(2, NKEY, NKEY, KD, P).transpose(0, 1, 4, 3, 2).reshape(2, NKEY, P, D),
        "v_tab": w["peer_v"].reshape(2, NKEY // GRP, GRP, NKEY, 4, 2 * P).transpose(0, 1, 4, 3, 2, 5).reshape(2, NKEY, P, D),
        "rg_in": chunks(w["rg_w_in"][0]),
        "gates": gates.reshape(8, P, D),
        "rg_out": chunks(w["rg_w_out"][0][:D]),
        "rg_tail": w["rg_w_out"][0][D:].reshape(2, P, D).transpose(1, 0, 2),
        "gla_state": w["state_gla"][0].transpose(0, 2, 1, 3).reshape(NB, P, D),
        "h_state": w["state_rglru_h"][0].reshape(NB, RT, P).transpose(2, 1, 0),
        "conv_state": w["state_rglru_conv"][0].reshape(NB, 3, RT, P).transpose(3, 2, 0, 1),
    }
    nc = bacc.Bacc("TRN2", target_bir_lowering=False, num_devices=1)
    feed, args = {}, []
    for name in _PARAMS:
        a = np.ascontiguousarray(arrays[name])
        feed[f"in_{name}"] = a
        args.append(nc.dram_tensor(f"in_{name}", a.shape, mybir.dt.from_np(a.dtype), kind="ExternalInput").ap())
    for name, shape in _OUTS:
        args.append(nc.dram_tensor(f"out_{name}", shape, F32, kind="ExternalOutput").ap())
    build_step(nc, *args)
    r = run_bass_kernel_spmd(nc, [feed], core_ids=[0]).results[0]
    y = r["out_y"].transpose(2, 1, 0).reshape(T, D)
    h = r["out_h"].transpose(2, 1, 0).reshape(NSEQ, DR)
    return (y[:SEQ].reshape(1, SEQ, D), y[SEQ:].reshape(NB, NT, D),
            r["out_gla_p"].transpose(1, 0, 2).reshape(1, 1, HEADS, P, HDV),
            r["out_gla_s"].reshape(1, NB, P, HEADS, HDV).transpose(0, 1, 3, 2, 4),
            h[:1].reshape(1, 1, DR), h[1:].reshape(1, NB, DR),
            r["out_conv_p"].transpose(2, 1, 0).reshape(1, 1, 3, DR),
            r["out_conv_s"].transpose(2, 3, 1, 0).reshape(1, NB, 3, DR))
```
